# Optimizing a Trainium2 kernel written in Bass

```python
import math
import jax, jax.numpy as jnp
from jax import lax
import numpy as np

D_MODEL = 2048
BATCH = 1
SEQ = 256
DEPTH = 2

N_MIXERS = 2
NSA_HEADS = 16
NSA_KV_GROUPS = 4
NSA_HEAD_DIM = D_MODEL // NSA_HEADS
CMP_BLOCK = 32
CMP_STRIDE = 16
SEL_BLOCK = 64
SEL_TOP_N = 8
WINDOW = 512
Q_BLOCK = 128
SEL_Q_BLOCK = 32
FORCE_SCORE = 1.0e4
HGRN_HEADS = 16
HGRN_KDIM = D_MODEL // HGRN_HEADS
HGRN_VDIM = D_MODEL // HGRN_HEADS
HGRN_CHUNK = 64
D_FF = 4 * D_MODEL
REL_BUCKETS = 32
REL_MAX_DIST = 128
RMS_EPS = 1e-6
NEG_INF = -1.0e30

kernel_name = "nsa_hgrn2_interleaved_trunk"

def rmsnorm(x, g):
    x32 = x.astype(jnp.float32)
    y = x32 * lax.rsqrt(jnp.mean(x32 * x32, axis=-1, keepdims=True) + RMS_EPS)
    return (y * g.astype(jnp.float32)).astype(x.dtype)

def rel_bucket(dist):
    n = jnp.maximum(dist, 0)
    max_exact = REL_BUCKETS // 2
    nf = jnp.maximum(n, 1).astype(jnp.float32)
    large = max_exact + (jnp.log(nf / max_exact) / math.log(REL_MAX_DIST / max_exact)
                         * (REL_BUCKETS - max_exact)).astype(jnp.int32)
    large = jnp.minimum(large, REL_BUCKETS - 1)
    return jnp.where(n < max_exact, n, large)

def compress_blocks(kraw, pe, w1, w2):
    B, S, G, Dh = kraw.shape
    ratio = CMP_BLOCK // CMP_STRIDE
    nh = S // CMP_STRIDE
    nc = nh - ratio + 1
    half = kraw.reshape(B, nh, CMP_STRIDE, G, Dh)
    blocks = jnp.concatenate([half[:, j:j + nc] for j in range(ratio)], axis=2)
    blocks = blocks + pe[:, None, :]
    flat = blocks.transpose(0, 1, 3, 2, 4).reshape(B, nc, G, CMP_BLOCK * Dh)
    return jax.nn.gelu(flat @ w1) @ w2

def nsa_mixer(h, w_in, cmp_pe, cmp_w1, cmp_w2, w_out, rel_table):
    B, S, _ = h.shape
    H, G, Dh = NSA_HEADS, NSA_KV_GROUPS, NSA_HEAD_DIM
    R = H // G
    dt = h.dtype
    proj = h @ w_in
    sizes = [H * Dh] + [G * Dh] * 6 + [3 * H]
    q, kc, vc, ks, vs, kw, vw, gl = jnp.split(proj, [int(v) for v in np.cumsum(sizes)[:-1]], axis=-1)
    q = q.reshape(B, S, G, R, Dh) * jnp.asarray(Dh ** -0.5, dt)
    kc, vc, ks, vs, kw, vw = [a.reshape(B, S, G, Dh) for a in (kc, vc, ks, vs, kw, vw)]
    gates = jax.nn.sigmoid(gl.astype(jnp.float32)).astype(dt).reshape(B, S, 3, G, R)
    pos = jnp.arange(S, dtype=jnp.int32)

    k_cmp = compress_blocks(kc, cmp_pe[0], cmp_w1[0], cmp_w2[0])
    v_cmp = compress_blocks(vc, cmp_pe[1], cmp_w1[1], cmp_w2[1])
    nc = k_cmp.shape[1]
    c_start = jnp.arange(nc, dtype=jnp.int32) * CMP_STRIDE
    c_end = c_start + CMP_BLOCK - 1
    dist_c = pos[:, None] - c_end[None, :]
    valid_c = dist_c >= 0
    bias_c = rel_table[rel_bucket(dist_c)].reshape(S, nc, G, R).transpose(2, 3, 0, 1)
    logit_c = jnp.einsum('bsgrd,bcgd->bgrsc', q, k_cmp).astype(jnp.float32) + bias_c
    logit_c = jnp.where(valid_c, logit_c, NEG_INF)
    any_c = jnp.any(valid_c, axis=-1).astype(jnp.float32)[:, None]
    p_c = jax.nn.softmax(logit_c, axis=-1) * any_c
    o_c = jnp.einsum('bgrsc,bcgd->bsgrd', p_c.astype(dt), v_cmp)

    nb = S // SEL_BLOCK
    jb = jnp.arange(nb, dtype=jnp.int32)
    b_start = jb * SEL_BLOCK
    overlap = ((c_start[:, None] <= b_start[None, :] + SEL_BLOCK - 1)
               & (c_end[:, None] >= b_start[None, :])).astype(jnp.float32)
    imp = jnp.einsum('bgrsc,cn->bgsn', p_c, overlap)
    q_blk = pos // SEL_BLOCK
    forced = (jb[None, :] == 0) | (jb[None, :] == q_blk[:, None]) | (jb[None, :] == q_blk[:, None] - 1)
    future = jb[None, :] > q_blk[:, None]
    imp = jnp.where(forced, FORCE_SCORE, jnp.where(future, -1.0, imp))
    n_sel = min(SEL_TOP_N, nb)
    _, sel_idx = lax.top_k(imp, n_sel)

    k_blk = ks.reshape(B, nb, SEL_BLOCK, G, Dh).transpose(0, 3, 1, 2, 4)
    v_blk = vs.reshape(B, nb, SEL_BLOCK, G, Dh).transpose(0, 3, 1, 2, 4)
    nqc = S // SEL_Q_BLOCK
    q_ch = q.reshape(B, nqc, SEL_Q_BLOCK, G, R, Dh).transpose(1, 0, 2, 3, 4, 5)
    idx_ch = sel_idx.reshape(B, G, nqc, SEL_Q_BLOCK, n_sel).transpose(2, 0, 1, 3, 4)
    t_ch = pos.reshape(nqc, SEL_Q_BLOCK)
    table_g = rel_table.reshape(REL_BUCKETS, G, R).transpose(1, 0, 2)
    bi = jnp.arange(B)[:, None, None, None]
    gi = jnp.arange(G)[None, :, None, None]
    gi5 = jnp.arange(G)[None, :, None, None, None]
    offs = jnp.arange(SEL_BLOCK, dtype=jnp.int32)

    def sel_step(args):
        qc, ic, tc = args
        kb = k_blk[bi, gi, ic]
        vb = v_blk[bi, gi, ic]
        kpos = ic[..., None] * SEL_BLOCK + offs
        dist = tc[None, None, :, None, None] - kpos
        bias = table_g[gi5, rel_bucket(dist)].transpose(0, 1, 5, 2, 3, 4)
        logit = jnp.einsum('btgrd,bgtnld->bgrtnl', qc, kb).astype(jnp.float32) + bias
        logit = jnp.where((dist >= 0)[:, :, None], logit, NEG_INF)
        sh = logit.shape
        p = jax.nn.softmax(logit.reshape(sh[:4] + (-1,)), axis=-1).reshape(sh)
        return jnp.einsum('bgrtnl,bgtnld->btgrd', p.astype(dt), vb)

    o_s = lax.map(sel_step, (q_ch, idx_ch, t_ch))
    o_s = o_s.transpose(1, 0, 2, 3, 4, 5).reshape(B, S, G, R, Dh)

    nqb = S // Q_BLOCK
    span = WINDOW + Q_BLOCK
    kw_p = jnp.pad(kw, ((0, 0), (WINDOW, 0), (0, 0), (0, 0)))
    vw_p = jnp.pad(vw, ((0, 0), (WINDOW, 0), (0, 0), (0, 0)))
    q_wb = q.reshape(B, nqb, Q_BLOCK, G, R, Dh).transpose(1, 0, 2, 3, 4, 5)

    def win_step(args):
        qb, c = args
        start = c * Q_BLOCK
        kb = lax.dynamic_slice_in_dim(kw_p, start, span, axis=1)
        vb = lax.dynamic_slice_in_dim(vw_p, start, span, axis=1)
        tq = start + jnp.arange(Q_BLOCK, dtype=jnp.int32)
        kp = start - WINDOW + jnp.arange(span, dtype=jnp.int32)
        dist = tq[:, None] - kp[None, :]
        valid = (dist >= 0) & (dist < WINDOW) & (kp[None, :] >= 0)
        bias = rel_table[rel_bucket(dist)].reshape(Q_BLOCK, span, G, R).transpose(2, 3, 0, 1)
        logit = jnp.einsum('btgrd,bsgd->bgrts', qb, kb).astype(jnp.float32) + bias
        logit = jnp.where(valid, logit, NEG_INF)
        p = jax.nn.softmax(logit, axis=-1)
        return jnp.einsum('bgrts,bsgd->btgrd', p.astype(dt), vb)

    o_w = lax.map(win_step, (q_wb, jnp.arange(nqb, dtype=jnp.int32)))
    o_w = o_w.transpose(1, 0, 2, 3, 4, 5).reshape(B, S, G, R, Dh)

    o = (gates[:, :, 0, :, :, None] * o_c + gates[:, :, 1, :, :, None] * o_s
         + gates[:, :, 2, :, :, None] * o_w)
    return o.reshape(B, S, H * Dh) @ w_out

def hgrn2_mixer(h, w_in, lb, onorm_g, w_out):
    B, S, D = h.shape
    H, dk, dv, C = HGRN_HEADS, HGRN_KDIM, HGRN_VDIM, HGRN_CHUNK
    dt = h.dtype
    proj = h @ w_in
    q, f, i, g = jnp.split(proj, 4, axis=-1)
    q = jax.nn.silu(q.astype(jnp.float32))
    f32 = f.astype(jnp.float32)
    lb = lb.astype(jnp.float32)
    log_f = jnp.logaddexp(jnp.log(lb), jnp.log1p(-lb) + jax.nn.log_sigmoid(f32))
    k = (1.0 - lb) * jax.nn.sigmoid(-f32)
    v = i.astype(jnp.float32)
    nch = S // C

    def to_chunks(a, d):
        return a.reshape(B, nch, C, H, d).transpose(1, 0, 3, 2, 4)

    qc_all, kc_all, vc_all = to_chunks(q, dk), to_chunks(k, dk), to_chunks(v, dv)
    b_all = jnp.cumsum(to_chunks(log_f, dk), axis=3)
    causal = jnp.tril(jnp.ones((C, C), dtype=bool))

    def step(state, args):
        qc, kc, vc, bc = args
        bl = bc[:, :, -1:, :]
        inter = jnp.einsum('bhtk,bhkv->bhtv', qc * jnp.exp(bc), state)
        decay = jnp.exp(jnp.where(causal[:, :, None],
                                  bc[:, :, :, None, :] - bc[:, :, None, :, :], -jnp.inf))
        a = jnp.einsum('bhtk,bhtsk,bhsk->bhts', qc, decay, kc)
        o = inter + jnp.einsum('bhts,bhsv->bhtv', a, vc)
        new_state = (jnp.exp(bl[:, :, 0, :, None]) * state
                     + jnp.einsum('bhsk,bhsv->bhkv', kc * jnp.exp(bl - bc), vc))
        return new_state, o

    s0 = jnp.zeros((B, H, dk, dv), jnp.float32)
    _, o = lax.scan(step, s0, (qc_all, kc_all, vc_all, b_all))
    o = o.transpose(1, 0, 3, 2, 4).reshape(B, S, H, dv)
    o = o * lax.rsqrt(jnp.mean(o * o, axis=-1, keepdims=True) + RMS_EPS)
    o = o.reshape(B, S, D) * onorm_g.astype(jnp.float32)
    o = o * jax.nn.silu(g.astype(jnp.float32))
    return o.astype(dt) @ w_out

def setup_inputs(seed: int = 0) -> dict:
    key = jax.random.key(seed)
    ks = jax.random.split(key, 16)
    n_a = (DEPTH + 1) // 2
    n_b = DEPTH // 2
    H, G, Dh = NSA_HEADS, NSA_KV_GROUPS, NSA_HEAD_DIM
    nsa_in = H * Dh + 6 * G * Dh + 3 * H
    nrm = lambda k, shape, fan: jax.random.normal(k, shape, jnp.float32) * (fan ** -0.5)
    return {
        "x": jax.random.normal(ks[0], (BATCH, SEQ, D_MODEL), jnp.float32),
        "norm_g": 1.0 + 0.02 * jax.random.normal(ks[1], (DEPTH, 4, D_MODEL), jnp.float32),
        "rel_table": 0.5 * jax.random.normal(ks[2], (REL_BUCKETS, NSA_HEADS), jnp.float32),
        "nsa_w_in": nrm(ks[3], (n_a, D_MODEL, nsa_in), D_MODEL),
        "nsa_cmp_pe": 0.1 * jax.random.normal(ks[4], (n_a, 2, CMP_BLOCK, Dh), jnp.float32),
        "nsa_cmp_w1": nrm(ks[5], (n_a, 2, CMP_BLOCK * Dh, Dh), CMP_BLOCK * Dh),
        "nsa_cmp_w2": nrm(ks[6], (n_a, 2, Dh, Dh), Dh),
        "nsa_w_out": nrm(ks[7], (n_a, H * Dh, D_MODEL), H * Dh),
        "hgrn_w_in": nrm(ks[8], (n_b, D_MODEL, 4 * D_MODEL), D_MODEL),
        "hgrn_lb": 0.1 * jax.random.normal(ks[9], (DEPTH, D_MODEL), jnp.float32),
        "hgrn_onorm": 1.0 + 0.02 * jax.random.normal(ks[10], (n_b, D_MODEL), jnp.float32),
        "hgrn_w_out": nrm(ks[11], (n_b, D_MODEL, D_MODEL), D_MODEL),
        "mlp_w_up": nrm(ks[12], (DEPTH, D_MODEL, D_FF), D_MODEL),
        "mlp_w_down": nrm(ks[13], (DEPTH, D_FF, D_MODEL), D_FF),
    }

def reference(x, norm_g, rel_table, nsa_w_in, nsa_cmp_pe, nsa_cmp_w1, nsa_cmp_w2, nsa_w_out,
              hgrn_w_in, hgrn_lb, hgrn_onorm, hgrn_w_out, mlp_w_up, mlp_w_down):
    lbs = jnp.cumsum(jax.nn.softmax(hgrn_lb.astype(jnp.float32), axis=0), axis=0)
    lbs = lbs - lbs[0:1]
    for layer in range(DEPTH):
        j = layer // N_MIXERS
        hn = rmsnorm(x, norm_g[layer, 0])
        if layer % N_MIXERS == 0:
            y = nsa_mixer(hn, nsa_w_in[j], nsa_cmp_pe[j], nsa_cmp_w1[j], nsa_cmp_w2[j],
                          nsa_w_out[j], rel_table)
        else:
            y = hgrn2_mixer(hn, hgrn_w_in[j], lbs[layer], hgrn_onorm[j], hgrn_w_out[j])
        x = x + rmsnorm(y, norm_g[layer, 1])
        hn = rmsnorm(x, norm_g[layer, 2])
        y = jnp.square(jax.nn.relu(hn @ mlp_w_up[layer])) @ mlp_w_down[layer]
        x = x + rmsnorm(y, norm_g[layer, 3])
    return x


_drawn_inputs = setup_inputs


def setup_inputs(seed=0):
    import zlib

    import numpy as np

    out = dict(_drawn_inputs(seed))
    spreads = {}
    factors = {'hgrn_lb': 8.0, 'hgrn_onorm': 5.592}
    for name, (base, spread) in spreads.items():
        noise = np.random.default_rng([zlib.crc32(name.encode()), seed]).standard_normal(out[name].shape)
        drawn = base * np.exp(spread * noise) if base else spread * noise
        out[name] = __import__('jax').numpy.asarray(drawn.astype(out[name].dtype))
    for name, factor in factors.items():
        out[name] = (out[name] * factor).astype(out[name].dtype)
    return out
```

```python
from contextlib import ExitStack

import numpy as np

import concourse.bass as bass
from concourse import mybir

ALU = mybir.AluOpType
ACT = mybir.ActivationFunctionType
AX = mybir.AxisListType
F32 = mybir.dt.float32
F32R = mybir.dt.float32r
BF16 = mybir.dt.bfloat16
U32 = mybir.dt.uint32

FULL = True
P = 128
EPS = 1e-6
NEG = -1.0e30
TINY = 1.0e-18
BUCKETS = 32
MAX_DIST = 128
CMP_BLOCK = 32
CMP_STRIDE = 16
LEVELS = 7
CHUNK = 64

RING = 4
SLOT = 2048
ACT_STEPS, DVE_STEPS = 8, 5
GATED_PARTS = (1, 0, 2, 3)
PIECE = 1024
SPLITS = 4
PIECES = RING * SLOT // PIECE
AHEAD = 3


def trunk_kernel(nc, x, norm_g, rel_table, nsa_w_in, nsa_cmp_pe, nsa_cmp_w1, nsa_cmp_w2, nsa_w_out,
                 hgrn_w_in, hgrn_lb, hgrn_onorm, hgrn_w_out, mlp_w_up, mlp_w_down,
                 identity, bucket_rows, bucket_rows_back, any_cmp, level_masks, out):
    S, D = x.shape[1], x.shape[2]
    TOK = S // P
    KT = D // P
    F = mlp_w_up.shape[2]
    H = rel_table.shape[1]
    G = ((nsa_w_in.shape[2] - 3 * H) // P - H) // 6
    R = H // G
    NC = S // CMP_STRIDE - CMP_BLOCK // CMP_STRIDE + 1
    COLS = 512
    QKV = (H + 6 * G) * P
    assert TOK == 2 and KT == 16 and H == 16 and G == 4 and QKV == 5120 and NC == 15
    SCALE = float(P) ** -0.5
    ND = 2 * S - 1

    N_IN, N_OUT, N_UP, N_GATED = QKV // COLS, D // COLS, F // COLS, 4 * D // COLS
    HALVES, DOWN_ROUNDS = 2, F // P // PIECES
    PR = {}
    n = 0
    for name, rounds in (("in", N_IN), ("out", N_OUT), ("up0", N_UP), ("down0", HALVES * DOWN_ROUNDS),
                         ("gated", N_GATED), ("out1", N_OUT), ("up1", N_UP), ("down1", HALVES * DOWN_ROUNDS)):
        PR[name] = n
        n += rounds
    WC = {}
    n = 0
    for name, chunks in (("in", N_IN), ("out", N_OUT), ("up0", N_UP), ("gated", N_GATED), ("out1", N_OUT),
                         ("up1", N_UP)):
        WC[name] = n
        n += chunks

    def raw_round(pr, name):
        return pr if name == "in" else pr + 1

    with ExitStack() as ctx:
        def sb(name, shape, dt=F32, stack=ctx):
            return stack.enter_context(nc.sbuf_tensor(name, shape, dt))

        def sem(name):
            return ctx.enter_context(nc.semaphore(name))

        def dram(name, shape):
            return nc.dram_tensor(name, shape, F32).ap()

        ps = ctx.enter_context(nc.psum_tensor("ps", [P, 8, COLS], F32))

        xs = sb("xs", [P, TOK, D])
        ys = sb("ys", [P, TOK, D])
        at_hi = sb("at_hi", [P, KT, S], F32R)
        at_lo = sb("at_lo", [P, KT, S], F32R)
        raw = sb("raw", [P, RING, SLOT])
        w_hi = sb("w_hi", [P, SPLITS, PIECE], F32R)
        w_lo = sb("w_lo", [P, SPLITS, PIECE], F32R)
        gain = sb("gain", [P, D])
        junk = sb("junk", [P, D // 2], BF16)
        ident = sb("ident", [P, P])
        gain_t = sb("gain_t", [P, P])
        ysq = sb("ysq", [P, TOK, N_OUT])
        ymean = sb("ymean", [P, TOK])
        yrstd = sb("yrstd", [P, TOK])
        xsq = sb("xsq", [P, TOK, 2])
        xmean = sb("xmean", [P, TOK])
        xrstd = sb("xrstd", [P, TOK])
        minus_half = sb("minus_half", [P, 8])
        relu_rows = sb("relu_rows", [P, TOK, COLS])
        misc_t = sb("misc_t", [P, 3 * KT])
        log_lb = sb("log_lb", [P, KT])
        log_rest = sb("log_rest", [P, KT])

        nsa = ExitStack()
        qkv = sb("qkv", [P, TOK, QKV], stack=nsa)
        q_t = sb("q_t", [P, R, S], stack=nsa)
        k_t = sb("k_t", [P, 2, S], stack=nsa)
        bias_cmp = sb("bias_cmp", [P, TOK, H, NC], stack=nsa)
        v_cmp = sb("v_cmp", [NC, G, P], stack=nsa)
        k_cmp = sb("k_cmp", [P, G * NC], stack=nsa)
        gate = sb("gate", [P, 3, TOK, H], stack=nsa)
        any_sb = sb("any_sb", [P, TOK], stack=nsa)
        stat = sb("stat", [P, 3, TOK, R], stack=nsa)
        total = sb("total", [P, 3, TOK, R], stack=nsa)
        weight = sb("weight", [P, 3, TOK, R], stack=nsa)
        p_cmp = sb("p_cmp", [P, TOK, R, NC], stack=nsa)
        early = ExitStack()
        wg_hi = sb("wg_hi", [P, KT, 3 * H], F32R, stack=early)
        wg_lo = sb("wg_lo", [P, KT, 3 * H], F32R, stack=early)
        early.close()
        v_cmp_now = sb("v_cmp_now", [NC, P], stack=nsa)
        p_t = sb("p_t", [P, 3, COLS], stack=nsa)
        nsa.close()
        gated = ExitStack()
        GT = R * S
        v_rows = sb("v_rows", [P, TOK, COLS], stack=gated)
        log_a = sb("log_a", [P, GT], stack=gated)
        log_b = sb("log_b", [P, GT], stack=gated)
        log_c = sb("log_c", [P, GT], stack=gated)
        key = sb("key", [P, GT], stack=gated)
        query = sb("query", [P, GT], stack=gated)
        run = sb("run", [P, GT], stack=gated)
        decay = sb("decay", [P, 2, GT], stack=gated)
        far_q = sb("far_q", [P, 2, GT // 2], stack=gated)
        mix_t = sb("mix_t", [P, R * TOK, P], stack=gated)
        cross_t = sb("cross_t", [P, R, P], stack=gated)
        gate_rows = sb("gate_rows", [P, TOK, COLS], stack=gated)
        restart = sb("restart", [P, GT], stack=gated)
        masks = sb("masks", [P, LEVELS, P // 2], stack=gated)
        lb_now = sb("lb_now", [P, R], stack=gated)
        rest_now = sb("rest_now", [P, R], stack=gated)
        last_sum = sb("last_sum", [P, R], stack=gated)
        osq = sb("osq", [P, TOK * R], stack=gated)
        orstd = sb("orstd", [P, TOK * R], stack=gated)
        gated.close()

        ys_flat = ys[:].rearrange("p t d -> p (t d)")
        logits = ys_flat[:, 0:6 * COLS].rearrange("p (b n c) -> p b n c", b=2, n=3)
        bias = ys_flat[:, 6 * COLS:8 * COLS].rearrange("p (h k) -> p h k", h=R)
        line_rows = ys_flat[:, 6 * COLS:7 * COLS]
        cmp_rows = ys_flat[:, 0:CMP_BLOCK * G * NC].rearrange("p (l g c) -> p l g c", l=CMP_BLOCK, g=G)
        kv0 = H * P
        staged_q = qkv[:, :, kv0:kv0 + R * P]
        staged_kv = qkv[:, :, kv0 + G * P:kv0 + 2 * G * P].rearrange("p t (s d) -> p t s d", s=4)
        rows_flat = relu_rows[:].rearrange("p t c -> p (t c)")
        wg_raw = rows_flat[:, 0:KT * 3 * H].rearrange("p (k n) -> p k n", k=KT)
        gain_rows = rows_flat[:, KT * 3 * H:KT * 3 * H + P]
        misc_rows = rows_flat[0:3 * KT, KT * 3 * H + P:KT * 3 * H + 2 * P]
        pc_t = rows_flat[0:NC, 0:R * S]
        p_cmp_flat = p_cmp[:].rearrange("p t h c -> p (t h c)")
        at = [0]

        def small(rows, cols):
            at[0] += cols
            return gain[0:rows, at[0] - cols:at[0]]

        rows_fwd = small(BUCKETS + 1, ND)
        rows_back = small(BUCKETS + 1, ND)
        table = small(BUCKETS + 1, H)
        pe_rows = small(2 * CMP_BLOCK, P)
        w2 = small(P, 2 * P).rearrange("p (i n) -> p i n", i=2)
        pe_t = small(P, 2 * CMP_BLOCK)
        gelu_z, gelu_u, gelu_e = (small(P, G * NC) for _ in range(3))
        gelu_out = small(P, 2 * G * NC).rearrange("p (i n) -> p i n", i=2)
        lb_tmp = small(P, 6 * KT).rearrange("p (i k) -> p i k", i=6)
        gate_tmp = small(P, TOK * 3 * H).rearrange("p (t n) -> p t n", t=TOK)

        def section(rows, t, h):
            return rows[:, 0, h * P:(h + 1) * P] if t == 0 else rows[:, 1 + h // 2, (h % 2) * S:(h % 2 + 1) * S]

        def section0(rows):
            return rows[:, 0, :].rearrange("p (h k) -> p h k", h=R)

        def p_t_of(b):
            return p_t[:].rearrange("p n c -> p (n c)") if b == 0 else logits[:, 0].rearrange("p n c -> p (n c)")

        mlp = ExitStack()
        hidden_t = sb("hidden_t", [P, F // P, S], stack=mlp)
        mlp.close()

        w_landed = [sem(f"w_landed{j}") for j in range(RING)]
        hi_ready = sem("hi_ready")
        lo_ready = sem("lo_ready")
        split_free = sem("split_free")
        acc_free = sem("acc_free")
        x_landed = sem("x_landed")
        const_landed = sem("const_landed")
        gain_landed = sem("gain_landed")
        gain_t_landed = sem("gain_t_landed")
        gain_t_turned = sem("gain_t_turned")
        gain_t_ready = sem("gain_t_ready")
        half_ready = sem("half_ready")
        x_ready = sem("x_ready")
        xt_ready = sem("xt_ready")
        at_hi_ready = sem("at_hi_ready")
        at_ready = sem("at_ready")
        xsq_ready = sem("xsq_ready")
        xmean_ready = sem("xmean_ready")
        xrstd_ready = sem("xrstd_ready")
        ysq_ready = sem("ysq_ready")
        y_seq = sem("y_seq")
        ymean_ready = sem("ymean_ready")
        yrstd_ready = sem("yrstd_ready")
        rows_turned = sem("rows_turned")
        hidden_ready = sem("hidden_ready")
        stored = sem("stored")
        wg_landed = sem("wg_landed")
        wg_hi_ready = sem("wg_hi_ready")
        wg_ready = sem("wg_ready")
        gate_acc = sem("gate_acc")
        gate_raw = sem("gate_raw")
        gate_exp = sem("gate_exp")
        gate_ready = sem("gate_ready")
        table_landed = sem("table_landed")
        table_ready = sem("table_ready")
        line_acc = sem("line_acc")
        line_ready = sem("line_ready")
        line_stored = sem("line_stored")
        square_stored = sem("square_stored")
        bias_cmp_acc = sem("bias_cmp_acc")
        bias_cmp_ready = sem("bias_cmp_ready")
        pe_rows_landed = sem("pe_rows_landed")
        pe_turned = sem("pe_turned")
        pe_t_ready = sem("pe_t_ready")
        raw_kv_turned = sem("raw_kv_turned")
        cmp_rows_ready = sem("cmp_rows_ready")
        cmp_done = sem("cmp_done")
        gelu_exp = sem("gelu_exp")
        gelu_in = sem("gelu_in")
        gelu_ready = sem("gelu_ready")
        cmp_out = sem("cmp_out")
        cmp_ready = sem("cmp_ready")
        small_seq = sem("small_seq")
        bias_landed = sem("bias_landed")
        q_staged = sem("q_staged")
        kv_staged = sem("kv_staged")
        q_turned = sem("q_turned")
        k_turned = sem("k_turned")
        q_ready = sem("q_ready")
        k_ready = sem("k_ready")
        cmp_logits = sem("cmp_logits")
        logits_acc = sem("logits_acc")
        cmp_max = sem("cmp_max")
        max_ready = sem("max_ready")
        cmp_exp = sem("cmp_exp")
        exp_ready = sem("exp_ready")
        p_cmp_ready = sem("p_cmp_ready")
        p_ready = sem("p_ready")
        p_cmp_turned = sem("p_cmp_turned")
        p_turned = sem("p_turned")
        pc_t_ready = sem("pc_t_ready")
        p_t_ready = sem("p_t_ready")
        o_acc = sem("o_acc")
        o_hi_ready = sem("o_hi_ready")
        o_ready = sem("o_ready")
        grp_seq = sem("grp_seq")

        misc_landed = sem("misc_landed")
        misc_turned = sem("misc_turned")
        lb_in = sem("lb_in")
        lb_out = sem("lb_out")
        lb_ready = sem("lb_ready")
        masks_landed = sem("masks_landed")
        dve_waited = sem("dve_waited")
        pool_waited = sem("pool_waited")
        act_seq = sem("act_seq")
        dve_seq = sem("dve_seq")
        f_turned = sem("f_turned")
        f_log = sem("f_log")
        f_read = sem("f_read")
        odds_ready = sem("odds_ready")
        key_ready = sem("key_ready")
        odds_log = sem("odds_log")
        q_turned1 = sem("q_turned1")
        q_log = sem("q_log")
        q_min = sem("q_min")
        q_sigmoid = sem("q_sigmoid")
        query_ready = sem("query_ready")
        diag_acc = sem("diag_acc")
        diag_read = sem("diag_read")
        delta_ready = sem("delta_ready")
        decay_ready = sem("decay_ready")
        sides_ready = sem("sides_ready")
        level_acc = sem("level_acc")
        level_read = sem("level_read")
        gate_log = sem("gate_log")
        gate_min = sem("gate_min")
        gate_sigmoid = sem("gate_sigmoid")
        mix_acc = sem("mix_acc")
        osq_ready = sem("osq_ready")
        omean_ready = sem("omean_ready")
        orstd_ready = sem("orstd_ready")
        mix_ready = sem("mix_ready")

        class Steps:

            def __init__(self, engine, semaphore):
                self.engine, self.semaphore, self.before, self.base, self.n = engine, semaphore, 0, 0, 0

            def turn(self, i, per):
                if self.n:
                    self.before += self.n
                self.base, self.n = self.before + i * per, 0

            def leave(self, turns, per):
                assert self.n == per, (self.n, per)
                self.before += turns * per
                self.base, self.n = self.before, 0

            def link(self, done):
                self.n += 1
                done.then_inc(self.semaphore, 1)
                self.engine.wait_ge(self.semaphore, self.base + self.n)
                return done

        x_rows = x.rearrange("b (t p) d -> p (b t) d", p=P)
        out_rows = out.rearrange("b (t p) d -> p (b t) d", p=P)
        bias_line = dram("bias_line", (H, ND))
        bias_square = dram("bias_square", (H, P, S))

        def by_feature(w):
            return w.rearrange("(k p) n -> p k n", p=P)

        w_in, w_out = by_feature(nsa_w_in[0]), by_feature(nsa_w_out[0])
        w_gated, w_out1 = by_feature(hgrn_w_in[0]), by_feature(hgrn_w_out[0])
        w_up = [by_feature(mlp_w_up[i]) for i in range(2)]
        w_down = [by_feature(mlp_w_down[i]) for i in range(2)]

        def chunk_done(pr):
            return PIECES * pr + (PIECES + SPLITS)

        block = ctx.enter_context(nc.Block())

        @block.sync
        def _(sp):
            def wait_slot(j, pr):
                sp.wait_ge(lo_ready, PIECES * pr + (2 * j + 2 - PIECES))

            def load_wide(w, chunk, pr, ring_is_free=False):
                for j in range(RING):
                    if not ring_is_free:
                        wait_slot(j, pr)
                    sp.dma_start(raw[:, j, :].rearrange("p (k n) -> p k n", k=4),
                                 w[:, 4 * j:4 * j + 4, bass.ds(chunk * COLS, COLS)]).then_inc(w_landed[j], 16)

            def load_down(w, half, rnd, pr):
                cols = slice(half * 2 * COLS, (half + 1) * 2 * COLS)
                for j in range(RING):
                    wait_slot(j, pr)
                    sp.dma_start(raw[:, j, :].rearrange("p (k n) -> p k n", k=2),
                                 w[:, bass.ds(rnd * PIECES + 2 * j, 2), cols]).then_inc(w_landed[j], 16)

            def load_mlp(layer):
                with sp.Fori(0, N_UP) as i:
                    load_wide(w_up[layer], i, i + PR[f"up{layer}"])
                for half in range(HALVES):
                    with sp.Fori(0, DOWN_ROUNDS) as i:
                        load_down(w_down[layer], half, i, i + (PR[f"down{layer}"] + half * DOWN_ROUNDS))

            for t in range(TOK):
                sp.dma_start(xs[:, t, :], x_rows[:, t, :]).then_inc(x_landed, 16)
            load_wide(w_in, 0, 0, ring_is_free=True)
            with sp.Fori(1, N_IN) as i:
                load_wide(w_in, i, i)
            for j in range(RING):
                wait_slot(j, N_IN)
                w1 = nsa_cmp_w1[0, j // 2].rearrange("(l d) n -> d l n", d=P)
                sp.dma_start(raw[:, j, :].rearrange("p (l n) -> p l n", l=16),
                             w1[:, 16 * (j % 2):16 * (j % 2) + 16, :]).then_inc(w_landed[j], 16)
            sp.wait_ge(cmp_done, 2)
            load_wide(w_out, 0, PR["out"], ring_is_free=True)
            with sp.Fori(1, N_OUT) as i:
                load_wide(w_out, i, i + PR["out"])
            load_mlp(0)
            if FULL:
                with sp.Fori(0, G) as g:
                    for kind, part in enumerate(GATED_PARTS):
                        load_wide(w_gated, g + part * N_OUT, g * 4 + (PR["gated"] + kind))
                with sp.Fori(0, N_OUT) as i:
                    load_wide(w_out1, i, i + PR["out1"])
                load_mlp(1)
            last = 3 if FULL else 1
            for n in range(N_OUT):
                sp.wait_ge(x_ready, N_OUT * last + n + 1)
                cols = slice(n * COLS, (n + 1) * COLS)
                sp.dma_start(out_rows[:, :, cols], xs[:, :, cols]).then_inc(stored, 16)
            sp.wait_ge(stored, 16 * N_OUT)

        @block.gpsimd
        def _(pool):
            def load_gain(layer, norm):
                pool.dma_start(gain[:], bass.AP(norm_g.tensor, (layer * 4 + norm) * D, [[0, P], [1, D]])
                               ).then_inc(gain_landed, 16)

            def x_factor(k):
                pool.wait_ge(xsq_ready, 2 * TOK * (k + 1))
                nc.gpsimd.tensor_tensor(xmean[:], xsq[:, :, 0], xsq[:, :, 1], ALU.add).then_inc(xmean_ready, 1)
                pool.wait_ge(xmean_ready, 2 * k + 1)
                nc.gpsimd.tensor_scalar(xmean[:], xmean[:], 1.0 / D, EPS, ALU.mult, ALU.add).then_inc(xmean_ready, 1)
                pool.wait_ge(xmean_ready, 2 * k + 2)
                nc.gpsimd.tensor_tensor(xrstd[:], xmean[:], minus_half[:, 0:TOK], ALU.pow).then_inc(xrstd_ready, 1)

            def y_factor(u):
                pool.wait_ge(ymean_ready, u + 1)
                nc.gpsimd.tensor_tensor(yrstd[:], ymean[:], minus_half[:, 0:TOK], ALU.pow).then_inc(yrstd_ready, 1)

            pool.sem_inc(orstd_ready, 1)
            nc.gpsimd.memset(minus_half[:], -0.5).then_inc(half_ready, 1)
            pool.wait_ge(half_ready, 1)
            pool.dma_start(ident[:], identity).then_inc(const_landed, 16)
            pool.dma_start(gain_rows, norm_g.rearrange("l n (k p) -> (l n k) p", p=P)).then_inc(gain_t_landed, 16)
            pool.dma_start(misc_rows[0:2 * KT, :], hgrn_lb.rearrange("l (k p) -> (l k) p", p=P)).then_inc(misc_landed, 16)
            pool.dma_start(misc_rows[2 * KT:3 * KT, :], hgrn_onorm[0].rearrange("(k p) -> k p", p=P)
                           ).then_inc(misc_landed, 16)
            nc.gpsimd.memset(table, 1.0).then_inc(table_landed, 1)
            pool.wait_ge(table_landed, 1)
            pool.dma_start(table[0:BUCKETS, :], rel_table).then_inc(table_ready, 16)
            pool.dma_start(rows_fwd, bucket_rows).then_inc(table_ready, 16)
            pool.dma_start(rows_back, bucket_rows_back).then_inc(table_ready, 16)
            pool.dma_start(pe_rows, nsa_cmp_pe[0].rearrange("i l d -> (i l) d")).then_inc(pe_rows_landed, 16)
            pool.dma_start(w2, nsa_cmp_w2[0].rearrange("i k n -> k i n")).then_inc(pe_rows_landed, 16)
            pool.dma_start(any_sb[:], any_cmp).then_inc(pe_rows_landed, 16)
            pool.dma_start(wg_raw, w_in[:, :, QKV:QKV + 3 * H]).then_inc(wg_landed, 16)
            x_factor(0)
            pool.wait_ge(line_ready, 1)
            pool.dma_start(bias_line, line_rows[0:H, 0:ND]).then_inc(line_stored, 16)
            pool.wait_ge(line_stored, 16)
            pool.dma_start(bias_square, bass.AP(bias_line.tensor, P - 1, [[ND, H], [-1, P], [1, S]])
                           ).then_inc(square_stored, 16)
            pool.wait_ge(square_stored, 16)
            with pool.Fori(0, G) as g:
                pool.wait_ge(max_ready, 2 * g + 1)
                pool.dma_start(bias, bias_square[bass.ds(g * R, R)].rearrange("h p k -> p h k")
                               ).then_inc(bias_landed, 16)
            pool.wait_ge(cmp_ready, 2)
            load_gain(0, 1)
            y_factor(0)
            x_factor(1)
            pool.wait_ge(x_ready, N_OUT)
            load_gain(0, 3)
            y_factor(1)
            if FULL:
                x_factor(2)
                pool.wait_ge(x_ready, 2 * N_OUT)
                pool.dma_start(masks[:], level_masks).then_inc(masks_landed, 16)
                load_gain(1, 1)
                with pool.Fori(0, G) as g:
                    pool.wait_ge(osq_ready, g + 1)
                    pool.sem_inc(pool_waited, 1)
                    nc.gpsimd.tensor_scalar(osq[:], osq[:], 1.0 / P, EPS, ALU.mult, ALU.add).then_inc(omean_ready, 1)
                    pool.wait_ge(omean_ready, g + 1)
                    nc.gpsimd.tensor_tensor(orstd[:], osq[:], minus_half[:], ALU.pow).then_inc(orstd_ready, 1)
                y_factor(2)
                x_factor(3)
                pool.wait_ge(x_ready, 3 * N_OUT)
                load_gain(1, 3)
                y_factor(3)

        @block.scalar
        def _(act):
            scalar = nc.scalar
            junk_user = []

            def own_junk():
                if junk_user:
                    act.wait_ge(*junk_user[-1])

            def split_hi(p, pr, rr):
                j = p // 2
                if p % 2 == 0:
                    act.wait_ge(w_landed[j], 16 * rr + 16)
                act.wait_ge(split_free, PIECES * pr + (p + 1))
                scalar.copy(w_hi[:, p % SPLITS, :], raw[:, j, (p % 2) * PIECE:(p % 2 + 1) * PIECE]
                            ).then_inc(hi_ready, 1)

            def wide_chunk(pr, rr, between, early=lambda p: None):
                for p in range(PIECES):
                    if p < AHEAD:
                        early(p)
                    if p == AHEAD:
                        between()
                    split_hi(p, pr, rr)

            def down_round(half, rnd, pr, between):
                for p in range(PIECES):
                    if p == AHEAD:
                        between()
                    if p % 2 == 0:
                        act.wait_ge(w_landed[p // 2], 16 * pr + 32)
                    act.wait_ge(split_free, PIECES * pr + (p + 1))
                    scalar.copy(at_hi[:, p:p + 1, :], hidden_t[:, bass.ds(rnd * PIECES + p, 1), :])
                    scalar.copy(w_hi[:, p % SPLITS, :], raw[:, p // 2, (p % 2) * PIECE:(p % 2 + 1) * PIECE]
                                ).then_inc(hi_ready, 1)

            def turn_in(b, columns):
                for f in range(KT // 2):
                    act.wait_ge(xt_ready, 8 * b + f + 1)
                    for k in range(2):
                        done = scalar.activation(at_hi[:, 2 * f + k, :], ps[:, 4 + f % 4, k * S:(k + 1) * S],
                                                 ACT.Copy, scale=columns[:, 2 * f + k:2 * f + k + 1])
                    done.then_inc(at_hi_ready, 1)

            def squares_of_x(k):
                for n in range(2 * TOK):
                    own_junk()
                    scalar.activation(junk[:], xs[:, n // 2, (n % 2) * D // 2:(n % 2 + 1) * D // 2], ACT.Square,
                                      accum_out=xsq[:, n // 2, n % 2:n % 2 + 1]).then_inc(xsq_ready, 1)
                    junk_user.append((xsq_ready, 2 * TOK * k + n + 1))

            def squares_of_y(u, n, banks, pr):
                act.wait_ge(split_free, chunk_done(pr))
                for t in range(TOK):
                    own_junk()
                    scalar.activation(junk[:, 0:COLS], ps[:, banks[t], :], ACT.Square,
                                      accum_out=ysq[:, t, n:n + 1]).then_inc(ysq_ready, 1)
                    junk_user.append((ysq_ready, 2 * N_OUT * u + 2 * n + t + 1))

            def square_hidden(u, chunk):
                act.wait_ge(rows_turned, u + 2)
                scalar.activation(hidden_t[:, bass.ds(chunk * 4, 4), :].rearrange("p k s -> p (k s)"),
                                  ps[:, 4:6, :].rearrange("p b c -> p (b c)"), ACT.Square).then_inc(hidden_ready, 1)

            def wide_rows_out(name, u, boundary, early=lambda p: None):
                for c in range(N_OUT):
                    pr = PR[name] + c
                    wide_chunk(pr, pr + 1, boundary if c == 0 else
                               lambda: squares_of_y(u, c - 1, [2 * ((c - 1) % 2), 2 * ((c - 1) % 2) + 1], pr - 1),
                               early if c == 0 else lambda p: None)

            def mlp_layer(layer, boundary):
                up, down = PR[f"up{layer}"], PR[f"down{layer}"]
                u0 = layer * N_UP

                def up_chunk(c, between_piece):
                    for p in range(PIECES):
                        if p == AHEAD and between_piece is boundary:
                            boundary()
                        if p == AHEAD + 3 and between_piece is not boundary:
                            between_piece()
                        split_hi(p, c + up, c + (up + 1))

                up_chunk(0, boundary)
                with act.Fori(0, N_UP // 2 - 1) as i:
                    for k in (1, 2):
                        up_chunk(i * 2 + k, lambda: square_hidden(i * 2 + (u0 + k - 1), i * 2 + (k - 1)))
                up_chunk(N_UP - 1, lambda: square_hidden(u0 + N_UP - 2, N_UP - 2))
                act.wait_ge(hidden_ready, u0 + N_UP)
                u = 2 * layer + 1

                def last_hidden():
                    square_hidden(u0 + N_UP - 1, N_UP - 1)
                    act.wait_ge(hidden_ready, u0 + N_UP + 1)

                down_round(0, 0, down, last_hidden)
                with act.Fori(1, DOWN_ROUNDS) as i:
                    down_round(0, i, i + down, lambda: None)
                pr = down + DOWN_ROUNDS

                def first_half():
                    for n in range(2):
                        squares_of_y(u, n, [2 * n, 2 * n + 1], pr - 1)

                down_round(1, 0, pr, first_half)
                with act.Fori(1, DOWN_ROUNDS) as i:
                    down_round(1, i, i + pr, lambda: None)

            def second_half(u, pr):
                for n in range(2):
                    squares_of_y(u, 2 + n, [4 + 2 * n, 5 + 2 * n], pr)

            def gains(layer, norm):
                return gain_t[:, (layer * 4 + norm) * KT:(layer * 4 + norm + 1) * KT]

            def turn_x(b, k, layer, norm):
                turn_in(b, gains(layer, norm))
                act.wait_ge(x_ready, N_OUT * k)
                squares_of_x(k)

            own = Steps(act, act_seq)

            def step(t, g):
                turned = ps[:, 4:6, :].rearrange("p b c -> p (b c)")
                if t == 13:
                    act.wait_ge(f_turned, g + 1)
                    own.link(scalar.activation(log_a[:], turned, ACT.Abs))
                if t == 14:
                    own.link(scalar.activation(log_a[:], log_a[:], ACT.Exp, scale=-1.0))
                if t == 15:
                    scalar.activation(log_a[:], log_a[:], ACT.Ln, bias=1.0).then_inc(f_log, 1)
                if t == 19:
                    act.wait_ge(f_read, g + 1)
                    for h in range(R):
                        done = scalar.activation(key[:, h * S:(h + 1) * S], log_c[:, h * S:(h + 1) * S], ACT.Exp,
                                                 scale=-1.0, bias=rest_now[:, h:h + 1])
                    done.then_inc(key_ready, 1)
                if t == 20:
                    act.wait_ge(odds_ready, g + 1)
                    own.link(scalar.activation(log_a[:], log_a[:], ACT.Abs))
                if t == 21:
                    own.link(scalar.activation(log_a[:], log_a[:], ACT.Exp, scale=-1.0))
                if t == 22:
                    scalar.activation(log_a[:], log_a[:], ACT.Ln, bias=1.0).then_inc(odds_log, 1)
                if t == 23:
                    act.wait_ge(key_ready, g + 1)
                    act.wait_ge(q_turned1, g + 1)
                    own.link(scalar.activation(log_c[:], turned, ACT.Abs))
                if t == 24:
                    own.link(scalar.activation(log_c[:], log_c[:], ACT.Exp, scale=-1.0))
                if t == 25:
                    scalar.activation(log_c[:], log_c[:], ACT.Ln, bias=1.0).then_inc(q_log, 1)
                if t == 27:
                    act.wait_ge(q_min, g + 1)
                    scalar.activation(log_c[:], log_c[:], ACT.Exp).then_inc(q_sigmoid, 1)
                if 29 <= t <= 29 + 2 * LEVELS and t % 2 == 1:
                    j = (t - 29) // 2
                    act.wait_ge(delta_ready, g * (LEVELS + 1) + (j + 1))
                    scalar.activation(decay[:, j % 2], decay[:, j % 2], ACT.Exp).then_inc(decay_ready, 1)
                if t == 37:
                    act.wait_ge(acc_free, g * 4 + (WC["gated"] + 3 + 3))
                    own.link(scalar.activation(gate_rows[:], relu_rows[:], ACT.Abs))
                if t == 38:
                    own.link(scalar.activation(gate_rows[:], gate_rows[:], ACT.Exp, scale=-1.0))
                if t == 39:
                    scalar.activation(gate_rows[:], gate_rows[:], ACT.Ln, bias=1.0).then_inc(gate_log, 1)
                if t == 41:
                    act.wait_ge(gate_min, g + 1)
                    scalar.activation(gate_rows[:], gate_rows[:], ACT.Exp).then_inc(gate_sigmoid, 1)
                if t == 49:
                    act.wait_ge(mix_acc, g + 1)
                    act.wait_ge(orstd_ready, g + 1)
                    own_junk()
                    for n in range(TOK * R):
                        done = scalar.activation(junk[:, n % 8 * P:(n % 8 + 1) * P],
                                                 ps[:, 6 + n // R, (n % R) * P:(n % R + 1) * P], ACT.Square,
                                                 accum_out=osq[:, n:n + 1])
                    done.then_inc(osq_ready, 1)

            def gated_layer():
                pr = PR["gated"]
                second_half_pr = PR["down0"] + HALVES * DOWN_ROUNDS - 1

                def into_gated():
                    second_half(1, second_half_pr)
                    turn_x(2, 2, 1, 0)

                def parts(g, before):
                    for c in range(4):
                        for p in range(PIECES):
                            t = 8 * c + p
                            if t == AHEAD and before is into_gated:
                                before()
                            step(t, g)
                            if before is not into_gated:
                                step(t + 32, before)
                            split_hi(p, g * 4 + (pr + c), g * 4 + (pr + c + 1))

                act.wait_ge(lb_ready, 1)
                parts(0, into_gated)
                with act.Fori(1, G) as g:
                    own.turn(g - 1, ACT_STEPS)
                    parts(g, g - 1)
                own.leave(G - 1, ACT_STEPS)

                def into_out1():
                    for t in range(32 + AHEAD, 64):
                        step(t, G - 1)
                    junk_user.append((osq_ready, G))
                    turn_in(3, misc_t[:, 2 * KT:3 * KT])

                wide_rows_out("out1", 2, into_out1, lambda p: step(32 + p, G - 1))

                def into_mlp1():
                    squares_of_y(2, N_OUT - 1, [2, 3], PR["out1"] + N_OUT - 1)
                    turn_x(4, 3, 1, 2)

                mlp_layer(1, into_mlp1)
                second_half(3, PR["down1"] + HALVES * DOWN_ROUNDS - 1)

            def start_in():
                act.wait_ge(gain_t_ready, 1)
                turn_in(0, gains(0, 0))

            act.sem_inc(hidden_ready, 1)
            act.wait_ge(lb_in, 1)
            scalar.activation(lb_tmp[:, 1:3], lb_tmp[:, 1:3], ACT.Exp).then_inc(lb_out, 1)
            act.wait_ge(lb_in, 2)
            scalar.activation(lb_tmp[:, 2:4], lb_tmp[:, 2:4], ACT.Ln).then_inc(lb_out, 1)
            act.wait_ge(x_landed, 16 * TOK)
            squares_of_x(0)
            wide_chunk(0, 0, start_in)
            with act.Fori(1, N_IN) as i:
                wide_chunk(i, i, lambda: None)

            def attention():
                act.wait_ge(wg_landed, 16)
                scalar.copy(wg_hi[:].rearrange("p k n -> p (k n)"), wg_raw.rearrange("p k n -> p (k n)")
                            ).then_inc(wg_hi_ready, 1)
                act.wait_ge(gate_raw, 1)
                scalar.activation(gate_tmp, gate_tmp, ACT.Exp, scale=-1.0).then_inc(gate_exp, 1)
                for i in range(2):
                    act.wait_ge(gelu_in, i + 1)
                    scalar.activation(gelu_e, gelu_u, ACT.Exp, scale=-2.0 * float(np.sqrt(2.0 / np.pi))
                                      ).then_inc(gelu_exp, 1)
                act.wait_ge(cmp_rows_ready, 2)
                act.wait_ge(raw_kv_turned, 2)
                with act.Fori(0, G) as g:
                    act.wait_ge(q_turned, g + 1)
                    scalar.copy(staged_q, qkv[:, :, bass.ds(g * R * P, R * P)]).then_inc(q_staged, 1)
                    act.wait_ge(q_turned, g + 2)
                    scalar.activation(q_t[:].rearrange("p h s -> p (h s)"),
                                      ps[:, 4:6, :].rearrange("p b c -> p (b c)"), ACT.Copy, scale=SCALE
                                      ).then_inc(q_ready, 1)
                    act.wait_ge(cmp_max, g + 1)
                    scalar.activation(p_cmp_flat, p_cmp_flat, ACT.Exp).then_inc(cmp_exp, 1)
                    for b in range(2):
                        act.wait_ge(max_ready, g * 2 + (b + 1) + 1)
                        for t in range(TOK):
                            for h in range(R):
                                row = section(logits[:, b], t, h)
                                done = scalar.activation(row, row, ACT.Exp, bias=stat[:, b, t, h:h + 1],
                                                         accum_out=total[:, b, t, h:h + 1])
                        done.then_inc(exp_ready, 1)
                    act.wait_ge(p_cmp_turned, g + 1)
                    scalar.copy(pc_t, ps[0:NC, 6:8, :].rearrange("p b c -> p (b c)")).then_inc(pc_t_ready, 1)
                    act.wait_ge(p_turned, g * 2 + 1)
                    scalar.copy(p_t_of(0), ps[:, 0:3, :].rearrange("p b c -> p (b c)")).then_inc(p_t_ready, 1)
                    act.wait_ge(p_turned, g * 2 + 2)
                    scalar.copy(p_t_of(1), ps[:, 3:6, :].rearrange("p b c -> p (b c)")).then_inc(p_t_ready, 1)
                    act.wait_ge(o_acc, g + 2)
                    scalar.copy(at_hi[:, bass.ds(g * R, R), :].rearrange("p k s -> p (k s)"),
                                ps[:, 0:2, :].rearrange("p b c -> p (b c)")).then_inc(o_hi_ready, 1)

            attention()
            wide_rows_out("out", 0, lambda: None)
            pr = PR["out"] + N_OUT - 1

            def into_mlp0():
                squares_of_y(0, N_OUT - 1, [2, 3], pr)
                turn_x(1, 1, 0, 2)

            mlp_layer(0, into_mlp0)
            if FULL:
                gated_layer()
            else:
                second_half(1, PR["down0"] + HALVES * DOWN_ROUNDS - 1)

        @block.vector
        def _(dve):
            vector = nc.vector
            seq = [0]

            def chain(done):
                seq[0] += 1
                done.then_inc(small_seq, 1)
                dve.wait_ge(small_seq, seq[0])

            def split_lo(p, pr):
                dve.wait_ge(hi_ready, PIECES * pr + (p + 1))
                vector.tensor_tensor(w_lo[:, p % SPLITS, :], raw[:, p // 2, (p % 2) * PIECE:(p % 2 + 1) * PIECE],
                                     w_hi[:, p % SPLITS, :].bitcast(F32), ALU.subtract).then_inc(lo_ready, 1)

            def wide_chunk(pr, between, early=lambda p: None):
                for p in range(PIECES):
                    if p < AHEAD:
                        early(p)
                    if p == AHEAD:
                        between()
                    split_lo(p, pr)

            def down_round(rnd, pr, between):
                for p in range(PIECES):
                    if p == AHEAD:
                        between()
                    dve.wait_ge(hi_ready, PIECES * pr + (p + 1))
                    vector.tensor_tensor(at_lo[:, p, :], hidden_t[:, bass.ds(rnd * PIECES + p, 1), :].rearrange(
                        "p k s -> p (k s)"), at_hi[:, p, :].bitcast(F32), ALU.subtract)
                    vector.tensor_tensor(w_lo[:, p % SPLITS, :],
                                         raw[:, p // 2, (p % 2) * PIECE:(p % 2 + 1) * PIECE],
                                         w_hi[:, p % SPLITS, :].bitcast(F32), ALU.subtract).then_inc(lo_ready, 1)

            def y_rows(u, n, banks, pr, wide):
                cols = slice(n * COLS, (n + 1) * COLS)
                dve.wait_ge(gain_landed, 16 * (u + 1))
                for t in range(TOK):
                    dve.wait_ge(ysq_ready, 2 * N_OUT * u + 2 * n + t + 1)
                    done = vector.tensor_tensor(ys[:, t, cols], ps[:, banks[t], :], gain[:, cols], ALU.mult)
                    if wide and t == TOK - 1:
                        done.then_inc(acc_free, 1)
                    else:
                        done.then_inc(y_seq, 1)
                        y_count[0] += 1

            y_count = [0]

            def update_x(u, n, acc):
                cols = slice(n * COLS, (n + 1) * COLS)
                for t in range(TOK):
                    done = vector.scalar_tensor_tensor(out=xs[:, t, cols], in0=ys[:, t, cols],
                                                       scalar=yrstd[:, t:t + 1], in1=xs[:, t, cols],
                                                       op0=ALU.mult, op1=ALU.add)
                done.then_inc(x_ready, 1)

            def y_factor(u, acc):
                dve.wait_ge(y_seq, y_count[0])
                if acc:
                    dve.wait_ge(acc_free, acc)
                chain(vector.tensor_reduce(ymean[:], ysq[:], AX.X, ALU.add))
                vector.tensor_scalar(ymean[:], ymean[:], 1.0 / D, EPS, ALU.mult, ALU.add).then_inc(ymean_ready, 1)
                dve.wait_ge(yrstd_ready, u + 1)

            def turn_in(b, columns, step=lambda f: None):
                for f in range(KT // 2):
                    step(f)
                    dve.wait_ge(at_hi_ready, 8 * b + f + 1)
                    for k in range(2):
                        kt = 2 * f + k
                        done = vector.scalar_tensor_tensor(
                            out=at_lo[:, kt, :], in0=ps[:, 4 + f % 4, k * S:(k + 1) * S],
                            scalar=columns[:, kt:kt + 1], in1=at_hi[:, kt, :].bitcast(F32),
                            op0=ALU.mult, op1=ALU.subtract)
                    done.then_inc(at_ready, 1)

            def turn_x(b, u, layer, norm, acc):
                y_factor(u, acc)
                update_x(u, 0, acc)
                update_x(u, 1, acc)

                def step(f):
                    if f in (1, 3):
                        update_x(u, 2 + f // 2, acc)

                turn_in(b, gain_t[:, (layer * 4 + norm) * KT:(layer * 4 + norm + 1) * KT], step)

            def relu_of(wc, pr, u, k, parity):
                dve.wait_ge(split_free, chunk_done(pr))
                dve.wait_ge(xrstd_ready, k + 1)
                dve.wait_ge(rows_turned, u + 1)
                for t in range(TOK):
                    done = vector.tensor_scalar(relu_rows[:, t, :], ps[:, 2 * parity + t, :], xrstd[:, t:t + 1], 0.0,
                                                ALU.mult, ALU.max)
                done.then_inc(acc_free, 1)

            def mlp_layer(layer, k, boundary):
                up, down, wc = PR[f"up{layer}"], PR[f"down{layer}"], WC[f"up{layer}"]
                u0 = layer * N_UP

                wide_chunk(up, boundary)
                with dve.Fori(0, N_UP // 2 - 1) as i:
                    for j in (1, 2):
                        wide_chunk(i * 2 + (up + j), lambda: relu_of(None, i * 2 + (up + j - 1), i * 2 + (u0 + j - 1), k,
                                                                     (j - 1) % 2))
                wide_chunk(up + N_UP - 1, lambda: relu_of(None, up + N_UP - 2, u0 + N_UP - 2, k, 0))
                down_round(0, down, lambda: relu_of(None, up + N_UP - 1, u0 + N_UP - 1, k, 1))
                with dve.Fori(1, DOWN_ROUNDS) as i:
                    down_round(i, i + down, lambda: None)
                u, pr = 2 * layer + 1, down + DOWN_ROUNDS

                def first_half():
                    for n in range(2):
                        y_rows(u, n, [2 * n, 2 * n + 1], pr - 1, False)

                down_round(0, pr, first_half)
                with dve.Fori(1, DOWN_ROUNDS) as i:
                    down_round(i, i + pr, lambda: None)

            def second_half(u, pr):
                for n in range(2):
                    y_rows(u, 2 + n, [4 + 2 * n, 5 + 2 * n], pr, False)

            dve.sem_inc(acc_free, 2)
            for counted_from_one in (max_ready, o_ready):
                dve.sem_inc(counted_from_one, 1)

            dve.wait_ge(gain_t_turned, 1)
            vector.tensor_copy(gain_t[:], ps[:, 7, 0:P]).then_inc(gain_t_ready, 1)
            dve.wait_ge(line_acc, 1)
            vector.tensor_copy(line_rows[0:H, 0:ND], ps[0:H, 4, 0:ND]).then_inc(line_ready, 1)
            dve.wait_ge(bias_cmp_acc, 1)
            vector.tensor_copy(bias_cmp[:].rearrange("p t h c -> p t c h"),
                               ps[:, 5, 0:TOK * NC * H].rearrange("p (t c h) -> p t c h", t=TOK, c=NC)
                               ).then_inc(bias_cmp_ready, 1)
            dve.wait_ge(pe_turned, 1)
            vector.tensor_copy(pe_t, ps[:, 6, 0:2 * CMP_BLOCK]).then_inc(pe_t_ready, 1)

            own = Steps(dve, dve_seq)

            def part_rows(rows, part, g):
                dve.wait_ge(split_free, PIECES * 4 * g + chunk_done(PR["gated"] + part))
                dve.wait_ge(xrstd_ready, 3)
                for t in range(TOK):
                    done = vector.tensor_scalar(rows[:, t, :], ps[:, 2 * (part % 2) + t, :], xrstd[:, t:t + 1], None,
                                                ALU.mult)
                done.then_inc(acc_free, 1)

            def halves(a, m):
                blocks = a.rearrange("p (n two m) -> p n two m", two=2, m=m)
                return blocks[:, :, 0, :], blocks[:, :, 1, :]

            def delta(j, g):
                if j >= 2:
                    dve.wait_ge(level_acc, g * (LEVELS + 1) + (j - 1))
                to = decay[:, j % 2]
                if j < LEVELS:
                    m = CHUNK >> j
                    (first, second), (to_first, to_second) = halves(run[:], m), halves(to, m)
                    ends = first[:, :, m - 1:m].broadcast_to((P, GT // (2 * m), m))
                    vector.tensor_tensor(to_first, ends, first, ALU.subtract)
                    if m == CHUNK:
                        done = vector.tensor_copy(to_second, second)
                    else:
                        done = vector.tensor_tensor(to_second, second, ends, ALU.subtract)
                else:
                    chunks = run[:].rearrange("p (h c m) -> p h c m", c=4, m=CHUNK)
                    out_chunks = to.rearrange("p (h c m) -> p h c m", c=4, m=CHUNK)

                    def end(c):
                        return chunks[:, :, c, CHUNK - 1:CHUNK].broadcast_to((P, R, CHUNK))

                    own.link(vector.tensor_tensor(last_sum[:], chunks[:, :, 0, CHUNK - 1], chunks[:, :, 1, CHUNK - 1],
                                                  ALU.add))
                    vector.tensor_tensor(out_chunks[:, :, 0], last_sum[:].unsqueeze(2).broadcast_to((P, R, CHUNK)),
                                         chunks[:, :, 0], ALU.subtract)
                    vector.tensor_tensor(out_chunks[:, :, 1], end(1), chunks[:, :, 1], ALU.subtract)
                    vector.tensor_copy(out_chunks[:, :, 2], chunks[:, :, 2])
                    done = vector.tensor_tensor(out_chunks[:, :, 3], chunks[:, :, 3], end(2), ALU.add)
                done.then_inc(delta_ready, 1)

            def sides(j, g):
                dve.wait_ge(decay_ready, g * (LEVELS + 1) + (j + 1))
                m = CHUNK >> j if j < LEVELS else P
                (to_first, to_second), (keys, _), (_, queries) = (halves(a, m) for a in
                                                                  (decay[:, j % 2], key[:], query[:]))
                vector.tensor_tensor(to_first, to_first, keys, ALU.mult)
                far = to_second if j == LEVELS else far_q[:, j % 2].rearrange("p (n m) -> p n m", m=m)
                vector.tensor_tensor(far, to_second, queries, ALU.mult).then_inc(sides_ready, 1)

            def take_level(j, g):
                dve.wait_ge(level_acc, g * (LEVELS + 1) + (j + 1))
                if j < LEVELS:
                    dve.sem_inc(dve_waited, 1)
                    m = CHUNK >> j
                    n = CHUNK // m
                    where = masks[:, j].bitcast(U32).rearrange("p (n m) -> p n m", m=m).unsqueeze(1).broadcast_to((P, R * TOK, n, m))
                    done = vector.copy_predicated(
                        mix_t[:].rearrange("p a (n two m) -> p a n two m", two=2, m=m)[:, :, :, 1, :], where,
                        ps[:, 6 + j % 2, :].rearrange("p (a n m) -> p a n m", a=R * TOK, m=m))
                else:
                    done = vector.tensor_copy(cross_t[:].rearrange("p h t -> p (h t)"), ps[:, 7, :])
                done.then_inc(level_read, 1)

            def step(t, g):
                turned = ps[:, 4:6, :].rearrange("p b c -> p (b c)")
                if t == 11:
                    part_rows(relu_rows, 0, g)
                if t == 17:
                    vector.tensor_copy(lb_now[:], log_lb[:, bass.ds(g * R, R)])
                    vector.tensor_copy(rest_now[:], log_rest[:, bass.ds(g * R, R)])
                    dve.wait_ge(f_log, g + 1)
                    vector.scalar_tensor_tensor(out=log_b[:], in0=turned, scalar=0.0, in1=log_a[:], op0=ALU.min,
                                                op1=ALU.subtract)
                    vector.scalar_tensor_tensor(out=log_c[:], in0=turned, scalar=0.0, in1=log_a[:], op0=ALU.max,
                                                op1=ALU.add).then_inc(f_read, 1)
                if t == 18:
                    dve.wait_ge(f_read, g + 1)
                    for op1, to, signal in ((ALU.subtract, log_a, odds_ready), (ALU.max, log_b, dve_seq)):
                        for h in range(R):
                            cols = slice(h * S, (h + 1) * S)
                            done = vector.tensor_scalar(to[:, cols], log_b[:, cols], rest_now[:, h:h + 1],
                                                        lb_now[:, h:h + 1], ALU.add, op1)
                        if signal is odds_ready:
                            done.then_inc(odds_ready, 1)
                            dve.wait_ge(odds_ready, g + 1)
                        else:
                            own.link(done)
                if t == 19:
                    part_rows(relu_rows, 1, g)
                if t == 23:
                    dve.wait_ge(odds_log, g + 1)
                    own.link(vector.tensor_tensor(log_b[:], log_b[:], log_a[:], ALU.add))
                if t == 24:
                    own.link(vector.tensor_tensor_scan(run[:], restart[:], log_b[:], 0.0, ALU.mult, ALU.add))
                if t == 26:
                    dve.wait_ge(q_log, g + 1)
                    vector.scalar_tensor_tensor(out=log_c[:], in0=turned, scalar=0.0, in1=log_c[:], op0=ALU.min,
                                                op1=ALU.subtract).then_inc(q_min, 1)
                if t == 28:
                    dve.wait_ge(q_sigmoid, g + 1)
                    vector.tensor_tensor(query[:], turned, log_c[:], ALU.mult).then_inc(query_ready, 1)
                if t == 27:
                    part_rows(v_rows, 2, g)
                if t == 29:
                    dve.wait_ge(diag_acc, g + 1)
                    for n in range(2):
                        done = vector.tensor_tensor(mix_t[:, 4 * n:4 * n + 4],
                                                    ps[:, 6 + n, :].rearrange("p (a t) -> p a t", a=4),
                                                    ident[:].unsqueeze(1).broadcast_to((P, 4, P)), ALU.mult)
                    done.then_inc(diag_read, 1)
                if t == 35:
                    part_rows(relu_rows, 3, g)
                if t == 40:
                    dve.wait_ge(gate_log, g + 1)
                    vector.scalar_tensor_tensor(out=gate_rows[:], in0=relu_rows[:], scalar=0.0, in1=gate_rows[:],
                                                op0=ALU.min, op1=ALU.subtract).then_inc(gate_min, 1)
                if t == 42:
                    dve.wait_ge(gate_sigmoid, g + 1)
                    own.link(vector.tensor_tensor(gate_rows[:], gate_rows[:], relu_rows[:], ALU.mult))
                if t == 51:
                    dve.wait_ge(orstd_ready, g + 2)
                    for n in range(TOK * R):
                        t_, cols = n // R, slice((n % R) * P, (n % R + 1) * P)
                        done = vector.scalar_tensor_tensor(out=ys[:, t_, bass.ds(g * COLS + (n % R) * P, P)],
                                                           in0=ps[:, 6 + t_, cols], scalar=orstd[:, n:n + 1],
                                                           in1=gate_rows[:, t_, cols], op0=ALU.mult, op1=ALU.mult)
                    done.then_inc(mix_ready, 1)
                for j in range(LEVELS + 1):
                    if t == 30 + 2 * j:
                        sides(j, g)
                    if t == 32 + 2 * j:
                        take_level(j, g)
                for j in range(LEVELS + 1):
                    if t == 28 + 2 * j:
                        delta(j, g)

            def gated_layer():
                pr = PR["gated"]

                def into_gated():
                    second_half(1, pr - 1)
                    turn_x(2, 1, 1, 0, 0)
                    dve.wait_ge(lb_ready, 1)
                    own.link(vector.memset(restart[:], 1.0))
                    own.link(vector.memset(restart[:].rearrange("p (n m) -> p n m", m=CHUNK)[:, :, 0:1], 0.0))
                    dve.wait_ge(masks_landed, 16)

                def parts(g, before):
                    for c in range(4):
                        for p in range(PIECES):
                            t = 8 * c + p
                            if before is not into_gated:
                                step(t + 32, before)
                            elif t == AHEAD:
                                before()
                            step(t, g)
                            split_lo(p, g * 4 + (pr + c))

                parts(0, into_gated)
                with dve.Fori(1, G) as g:
                    own.turn(g - 1, DVE_STEPS)
                    parts(g, g - 1)
                own.leave(G - 1, DVE_STEPS)

                def into_out1():
                    for t in range(32 + AHEAD, 64):
                        step(t, G - 1)
                    turn_in(3, misc_t[:, 2 * KT:3 * KT])

                wide_rows_out("out1", 2, into_out1, lambda p: step(32 + p, G - 1))

                def into_mlp1():
                    y_rows(2, N_OUT - 1, [2, 3], PR["out1"] + N_OUT - 1, True)
                    turn_x(4, 2, 1, 2, 2 + WC["out1"] + N_OUT)

                mlp_layer(1, 3, into_mlp1)
                second_half(3, PR["down1"] + HALVES * DOWN_ROUNDS - 1)
                y_factor(3, 0)
                for n in range(N_OUT):
                    update_x(3, n, 0)

            dve.wait_ge(misc_turned, 1)
            chain(vector.tensor_copy(misc_t[:], ps[:, 3, 0:3 * KT]))
            low, high, top = misc_t[:, 0:KT], misc_t[:, KT:2 * KT], lb_tmp[:, 0]
            chain(vector.tensor_tensor(top, low, high, ALU.max))
            vector.tensor_tensor(lb_tmp[:, 1], low, top, ALU.subtract)
            vector.tensor_tensor(lb_tmp[:, 2], high, top, ALU.subtract).then_inc(lb_in, 1)
            dve.wait_ge(lb_out, 1)
            chain(vector.tensor_tensor(top, lb_tmp[:, 1], lb_tmp[:, 2], ALU.add))
            chain(vector.reciprocal(top, top))
            vector.tensor_tensor(lb_tmp[:, 1], lb_tmp[:, 1], top, ALU.mult)
            chain(vector.tensor_tensor(lb_tmp[:, 2], lb_tmp[:, 2], top, ALU.mult))
            chain(vector.tensor_tensor(lb_tmp[:, 2], lb_tmp[:, 1], lb_tmp[:, 2], ALU.add))
            chain(vector.tensor_tensor(lb_tmp[:, 2], lb_tmp[:, 2], lb_tmp[:, 1], ALU.subtract))
            chain(vector.tensor_scalar(lb_tmp[:, 3], lb_tmp[:, 2], -1.0, 1.0, ALU.mult, ALU.add))
            vector.tensor_scalar(lb_tmp[:, 4:6], lb_tmp[:, 2:4], TINY, NEG, ALU.is_lt, ALU.mult)
            chain(vector.tensor_scalar(lb_tmp[:, 0:2], lb_tmp[:, 2:4], TINY, None, ALU.max))
            vector.tensor_copy(lb_tmp[:, 2:4], lb_tmp[:, 0:2]).then_inc(lb_in, 1)
            dve.wait_ge(lb_out, 2)
            vector.tensor_tensor(log_lb[:], lb_tmp[:, 2], lb_tmp[:, 4], ALU.add)
            vector.tensor_tensor(log_rest[:], lb_tmp[:, 3], lb_tmp[:, 5], ALU.add).then_inc(lb_ready, 1)

            def qkv_rows(c, pr, parity):
                dve.wait_ge(split_free, chunk_done(pr))
                dve.wait_ge(xrstd_ready, 1)
                for t in range(TOK):
                    done = vector.tensor_scalar(qkv[:, t, bass.ds(c * COLS, COLS)], ps[:, 2 * parity + t, :],
                                                xrstd[:, t:t + 1], None, ALU.mult)
                done.then_inc(acc_free, 1)

            wide_chunk(0, lambda: turn_in(0, gain_t[:, 0:KT]))
            with dve.Fori(0, N_IN // 2 - 1) as i:
                for j in (1, 2):
                    wide_chunk(i * 2 + j, lambda: qkv_rows(i * 2 + (j - 1), i * 2 + (j - 1), (j - 1) % 2))
            wide_chunk(N_IN - 1, lambda: qkv_rows(N_IN - 2, N_IN - 2, 0))

            def gates():
                dve.wait_ge(wg_hi_ready, 1)
                vector.tensor_tensor(wg_lo[:], wg_raw, wg_hi[:].bitcast(F32), ALU.subtract).then_inc(wg_ready, 1)
                dve.wait_ge(gate_acc, 1)
                for t in range(TOK):
                    done = vector.tensor_scalar(gate_tmp[:, t], ps[:, 6, t * 3 * H:(t + 1) * 3 * H],
                                                xrstd[:, t:t + 1], None, ALU.mult)
                done.then_inc(gate_raw, 1)
                dve.wait_ge(gate_exp, 1)
                chain(vector.tensor_scalar(gate_tmp, gate_tmp, 1.0, None, ALU.add))
                chain(vector.reciprocal(gate_tmp, gate_tmp))
                for b in range(3):
                    done = vector.tensor_copy(gate[:, (b + 2) % 3], gate_tmp[:, :, b * H:(b + 1) * H])
                chain(done)
                dve.wait_ge(pe_rows_landed, 48)
                chain(vector.tensor_tensor(gate[:, 2], gate[:, 2], any_sb[:].unsqueeze(2).broadcast_to((P, TOK, H)),
                                           ALU.mult))

            def compress():
                for i in range(2):
                    dve.wait_ge(raw_kv_turned, i + 1)
                    if i == 1:
                        dve.wait_ge(cmp_done, 1)
                    for a in range(2):
                        for b in range(2):
                            halves = ps[:, 2 * i + b, :].rearrange("p (g c r) -> p r g c", g=2, r=CMP_STRIDE)
                            offsets = pe_t[:, i * CMP_BLOCK + a * CMP_STRIDE:i * CMP_BLOCK + (a + 1) * CMP_STRIDE]
                            for gg in range(2):
                                done = vector.tensor_tensor(
                                    cmp_rows[:, a * CMP_STRIDE:(a + 1) * CMP_STRIDE, 2 * b + gg, :],
                                    halves[:, :, gg, a:a + NC],
                                    offsets.unsqueeze(2).broadcast_to((P, CMP_STRIDE, NC)), ALU.add)
                    done.then_inc(cmp_rows_ready, 1)
                    dve.wait_ge(cmp_done, i + 1)
                    chain(vector.tensor_copy(gelu_z, ps[:, 4 + i, 0:G * NC]))
                    chain(vector.tensor_tensor(gelu_u, gelu_z, gelu_z, ALU.mult))
                    chain(vector.tensor_scalar(gelu_u, gelu_u, 0.044715, 1.0, ALU.mult, ALU.add))
                    vector.tensor_tensor(gelu_u, gelu_u, gelu_z, ALU.mult).then_inc(gelu_in, 1)
                    dve.wait_ge(gelu_exp, i + 1)
                    chain(vector.tensor_scalar(gelu_e, gelu_e, 1.0, None, ALU.add))
                    chain(vector.reciprocal(gelu_e, gelu_e))
                    vector.tensor_tensor(gelu_out[:, i], gelu_z, gelu_e, ALU.mult).then_inc(gelu_ready, 1)
                    dve.wait_ge(gelu_ready, i + 1)
                dve.wait_ge(cmp_out, 1)
                vector.tensor_copy(k_cmp[:], ps[:, 6, 0:G * NC]).then_inc(cmp_ready, 1)
                dve.wait_ge(cmp_out, 2)
                vector.tensor_copy(v_cmp[:].rearrange("c g d -> c (g d)"), ps[0:NC, 7, :]).then_inc(cmp_ready, 1)

            GRP = 13

            def group(g, start):
                n = [0]

                def link(done):
                    n[0] += 1
                    done.then_inc(grp_seq, 1)
                    dve.wait_ge(grp_seq, g * GRP + n[0])

                dve.wait_ge(o_acc, g + 1)
                vector.tensor_copy(v_cmp_now[:], v_cmp[:, bass.ds(g, 1), :].rearrange("c g d -> c (g d)"))
                for t in range(TOK):
                    rows = qkv[:, t, H * P + 2 * G * P:].rearrange("p (s n) -> p s n", s=4)
                    done = vector.tensor_copy(staged_kv[:, t], rows[:, :, bass.ds(g * P, P)])
                done.then_inc(kv_staged, 1)
                dve.wait_ge(k_turned, g + 1)
                vector.tensor_copy(k_t[:].rearrange("p b s -> p (b s)"), ps[:, 6, :]).then_inc(k_ready, 1)
                dve.wait_ge(cmp_logits, g + 1)
                link(vector.tensor_tensor(p_cmp[:], ps[:, 7, 0:TOK * R * NC].rearrange("p (t h c) -> p t h c", t=TOK, h=R),
                                          bias_cmp[:, :, bass.ds(g * R, R), :], ALU.add))
                link(vector.tensor_reduce(stat[:, 2], p_cmp[:], AX.X, ALU.max))
                over = lambda a: a.unsqueeze(3).broadcast_to((P, TOK, R, NC))
                vector.tensor_tensor(p_cmp[:], p_cmp[:], over(stat[:, 2]), ALU.subtract).then_inc(cmp_max, 1)
                dve.wait_ge(bias_landed, g * 16 + 16)
                for b in range(2):
                    dve.wait_ge(logits_acc, g * 2 + (b + 1))
                    low = section0(logits[:, b])
                    vector.tensor_tensor(low, ps[:, 3 * b, :].rearrange("p (h k) -> p h k", h=R), bias[:, :, P:S],
                                         ALU.add)
                    for m in range(2):
                        done = vector.tensor_tensor(
                            logits[:, b, 1 + m, :].rearrange("p (h k) -> p h k", h=2),
                            ps[:, 3 * b + 1 + m, :].rearrange("p (h k) -> p h k", h=2),
                            bias[:, 2 * m:2 * m + 2, :], ALU.add)
                    link(done)
                    vector.tensor_reduce(stat[:, b, 0], low, AX.X, ALU.max)
                    link(vector.tensor_reduce(stat[:, b, 1], logits[:, b, 1:3, :].rearrange(
                        "p m (h k) -> p (m h) k", h=2), AX.X, ALU.max))
                    vector.tensor_scalar(stat[:, b], stat[:, b], -1.0, None, ALU.mult).then_inc(max_ready, 1)
                dve.wait_ge(cmp_exp, g + 1)
                link(vector.tensor_reduce(total[:, 2], p_cmp[:], AX.X, ALU.add))
                link(vector.reciprocal(weight[:, 2], total[:, 2]))
                link(vector.tensor_tensor(weight[:, 2], weight[:, 2], gate[:, 2, :, bass.ds(g * R, R)], ALU.mult))
                vector.tensor_tensor(p_cmp[:], p_cmp[:], over(weight[:, 2]), ALU.mult).then_inc(p_cmp_ready, 1)
                for b in range(2):
                    dve.wait_ge(exp_ready, g * 2 + (b + 1))
                    link(vector.reciprocal(weight[:, b], total[:, b]))
                    link(vector.tensor_tensor(weight[:, b], weight[:, b], gate[:, b, :, bass.ds(g * R, R)], ALU.mult))
                    low = section0(logits[:, b])
                    vector.tensor_tensor(low, low, weight[:, b, 0].unsqueeze(2).broadcast_to((P, R, P)), ALU.mult)
                    for m in range(2):
                        high = logits[:, b, 1 + m, :].rearrange("p (h k) -> p h k", h=2)
                        done = vector.tensor_tensor(high, high, weight[:, b, 1, 2 * m:2 * m + 2].unsqueeze(2)
                                                    .broadcast_to((P, 2, S)), ALU.mult)
                    done.then_inc(p_ready, 1)
                dve.wait_ge(o_hi_ready, g + 1)
                vector.tensor_tensor(at_lo[:, bass.ds(g * R, R), :].rearrange("p k s -> p (k s)"),
                                     ps[:, 0:2, :].rearrange("p b c -> p (b c)"),
                                     at_hi[:, bass.ds(g * R, R), :].rearrange("p k s -> p (k s)").bitcast(F32),
                                     ALU.subtract).then_inc(o_ready, 1)
                return n[0]

            def attention():
                qkv_rows(N_IN - 1, N_IN - 1, 1)
                dve.wait_ge(acc_free, 2 + N_IN)
                gates()
                compress()
                dve.wait_ge(cmp_ready, 2)
                with dve.Fori(0, G) as g:
                    steps = group(g, 0)
                    assert steps == GRP, steps

            def wide_rows_out(name, u, boundary, early=lambda p: None):
                for c in range(N_OUT):
                    pr = PR[name] + c
                    wide_chunk(pr, boundary if c == 0 else
                               lambda: y_rows(u, c - 1, [2 * ((c - 1) % 2), 2 * ((c - 1) % 2) + 1], pr - 1, True),
                               early if c == 0 else lambda p: None)

            attention()
            wide_rows_out("out", 0, lambda: None)

            def into_mlp0():
                y_rows(0, N_OUT - 1, [2, 3], PR["out"] + N_OUT - 1, True)
                turn_x(1, 0, 0, 2, 2 + WC["out"] + N_OUT)

            mlp_layer(0, 1, into_mlp0)
            if FULL:
                gated_layer()
            else:
                second_half(1, PR["down0"] + HALVES * DOWN_ROUNDS - 1)
                y_factor(1, 0)
                for n in range(N_OUT):
                    update_x(1, n, 0)

        @block.tensor
        def _(pe):
            tensor = nc.tensor

            def three_passes(acc, kt, t, hi, lo, start, stop, a_slot=None):
                rows = slice(t * P, (t + 1) * P)
                tensor.matmul(acc, at_hi[:, kt, rows], hi, start=start, stop=False)
                tensor.matmul(acc, at_lo[:, kt, rows], hi, start=False, stop=False)
                return tensor.matmul(acc, at_hi[:, kt, rows], lo, start=False, stop=stop)

            def wide_chunk(pr, wc, parity, before=lambda p: None, after=lambda p: None):
                pe.wait_ge(acc_free, wc + 1)
                for p in range(PIECES):
                    before(p)
                    pe.wait_ge(lo_ready, PIECES * pr + (p + 1))
                    for k in range(2):
                        cols = slice(k * COLS, (k + 1) * COLS)
                        for t in range(TOK):
                            done = three_passes(ps[:, 2 * parity + t, :], 2 * p + k, t, w_hi[:, p % SPLITS, cols],
                                                w_lo[:, p % SPLITS, cols], p + k == 0, 2 * p + k == KT - 1)
                    done.then_inc(split_free, 1)
                    after(p)

            def down_round(half, pr, first, last, after=lambda p: None):
                for p in range(PIECES):
                    pe.wait_ge(lo_ready, PIECES * pr + (p + 1))
                    for n in range(2):
                        cols = slice(n * COLS, (n + 1) * COLS)
                        for t in range(TOK):
                            done = three_passes(ps[:, 4 * half + 2 * n + t, :], p, t, w_hi[:, p % SPLITS, cols],
                                                w_lo[:, p % SPLITS, cols], first and p == 0,
                                                last and p == PIECES - 1)
                    done.then_inc(split_free, 1)
                    after(p)

            def turn(b, f, source):
                if f >= 4:
                    pe.wait_ge(at_ready, 8 * b + f - 4 + 1)
                for k in range(2):
                    for t in range(TOK):
                        kt = 2 * f + k
                        done = tensor.transpose(ps[:, 4 + f % 4, k * S + t * P:k * S + (t + 1) * P],
                                                source[:, t, kt * P:(kt + 1) * P], ident[:])
                done.then_inc(xt_ready, 1)

            def turned_chunk(b, pr, wc, source, wait_source):
                def before(p):
                    for f in ((0, 1, 2, 3), (4, 5), (6, 7), (), (), (), (), ())[p]:
                        wait_source(f)
                        turn(b, f, source)
                    pe.wait_ge(at_ready, 8 * b + p + 1)
                wide_chunk(pr, wc, 0, before)

            def turn_hidden(wc, u):
                pe.wait_ge(acc_free, wc + 2)
                pe.wait_ge(hidden_ready, u + 1)
                for j in range(4):
                    for t in range(TOK):
                        done = tensor.transpose(ps[:, 4 + j // 2, (j % 2) * S + t * P:(j % 2) * S + (t + 1) * P],
                                                relu_rows[:, t, j * P:(j + 1) * P], ident[:])
                done.then_inc(rows_turned, 1)

            def mlp_layer(layer, b, update):
                up, down, wc, u0 = PR[f"up{layer}"], PR[f"down{layer}"], WC[f"up{layer}"], layer * N_UP
                turned_chunk(b, up, wc, xs, lambda f: pe.wait_ge(x_ready, N_OUT * update + f // 2 + 1))

                def at(piece, work):
                    return lambda p: work() if p == piece else None

                with pe.Fori(0, N_UP // 2 - 1) as i:
                    for j in (1, 2):
                        wide_chunk(i * 2 + (up + j), i * 2 + (wc + j), j % 2,
                                   after=at(1, lambda: turn_hidden(i * 2 + (wc + j), i * 2 + (u0 + j - 1))))
                wide_chunk(up + N_UP - 1, wc + N_UP - 1, 1,
                           after=at(1, lambda: turn_hidden(wc + N_UP - 1, u0 + N_UP - 2)))
                pe.wait_ge(acc_free, wc + N_UP + 2)
                down_round(0, down, True, False, after=at(1, lambda: turn_hidden(wc + N_UP, u0 + N_UP - 1)))
                with pe.Fori(1, DOWN_ROUNDS - 1) as i:
                    down_round(0, i + down, False, False)
                down_round(0, down + DOWN_ROUNDS - 1, False, True)
                down += DOWN_ROUNDS
                pe.wait_ge(hidden_ready, u0 + N_UP + 1)
                down_round(1, down, True, False)
                with pe.Fori(1, DOWN_ROUNDS - 1) as i:
                    down_round(1, i + down, False, False)
                down_round(1, down + DOWN_ROUNDS - 1, False, True)

            def turn_part(g, part, ready):
                pe.wait_ge(acc_free, g * 4 + (WC["gated"] + part + 3))
                for h in range(R):
                    for t in range(TOK):
                        done = tensor.transpose(ps[:, 4 + h // 2, (h % 2) * S + t * P:(h % 2) * S + (t + 1) * P],
                                                relu_rows[:, t, h * P:(h + 1) * P], ident[:])
                done.then_inc(ready, 1)

            def step(t, g):
                if t == 9:
                    pe.wait_ge(query_ready, g)
                    turn_part(g, 0, f_turned)
                if t == 18:
                    pe.wait_ge(f_read, g + 1)
                    turn_part(g, 1, q_turned1)
                if t == 25:
                    pe.wait_ge(key_ready, g + 1)
                    pe.wait_ge(query_ready, g + 1)
                    pe.wait_ge(mix_ready, g)
                    for a in range(R * TOK):
                        done = tensor.matmul(ps[:, 6 + a // 4, (a % 4) * P:(a % 4 + 1) * P], key[:, a * P:(a + 1) * P],
                                             query[:, a * P:(a + 1) * P], start=True, stop=True)
                    done.then_inc(diag_acc, 1)
                if 27 <= t <= 27 + 2 * LEVELS and t % 2 == 1:
                    j = (t - 27) // 2
                    pe.wait_ge(sides_ready, g * (LEVELS + 1) + (j + 1))
                    pe.wait_ge(diag_read, g + 1)
                    if j >= 2:
                        pe.wait_ge(level_read, g * (LEVELS + 1) + (j - 1))
                    if j < LEVELS:
                        half = P // 2
                        for a in range(R * TOK):
                            done = tensor.matmul(ps[:, 6 + j % 2, a * half:(a + 1) * half],
                                                 decay[:, j % 2, a * P:(a + 1) * P],
                                                 far_q[:, j % 2, a * half:(a + 1) * half], start=True, stop=True)
                    else:
                        for h in range(R):
                            done = tensor.matmul(ps[:, 7, h * P:(h + 1) * P], decay[:, 1, h * S:h * S + P],
                                                 decay[:, 1, h * S + P:(h + 1) * S], start=True, stop=True)
                    done.then_inc(level_acc, 1)
                if t == 44:
                    pe.wait_ge(level_read, g * (LEVELS + 1) + (LEVELS + 1))
                    pe.wait_ge(acc_free, g * 4 + (WC["gated"] + 2 + 3))
                    for h in range(R):
                        cols = slice(h * P, (h + 1) * P)
                        tensor.matmul(ps[:, 6, cols], mix_t[:, h * TOK, :], v_rows[:, 0, cols], start=True, stop=True)
                        tensor.matmul(ps[:, 7, cols], cross_t[:, h, :], v_rows[:, 0, cols], start=True, stop=False)
                        done = tensor.matmul(ps[:, 7, cols], mix_t[:, h * TOK + 1, :], v_rows[:, 1, cols],
                                             start=False, stop=True)
                    done.then_inc(mix_acc, 1)

            def gated_layer():
                pr, wc = PR["gated"], WC["gated"]
                for c in range(4):
                    after = lambda p: step(8 * c + p, 0)
                    if c == 0:
                        turned_chunk(2, pr, wc, xs, lambda f: pe.wait_ge(x_ready, N_OUT + f // 2 + 1))
                    else:
                        wide_chunk(pr + c, wc + c, c % 2, after=after)
                with pe.Fori(1, G) as g:
                    for c in range(4):
                        def after(p):
                            step(8 * c + p + 32, g - 1)
                            step(8 * c + p, g)
                        wide_chunk(g * 4 + (pr + c), g * 4 + (wc + c), c % 2, after=after)
                for t in range(32, 64):
                    step(t, G - 1)
                turned_chunk(3, PR["out1"], WC["out1"], ys, lambda f: pe.wait_ge(mix_ready, G))
                for c in range(1, N_OUT):
                    wide_chunk(PR["out1"] + c, WC["out1"] + c, c % 2)
                mlp_layer(1, 4, 2)

            pe.sem_inc(split_free, SPLITS)
            for counted_from_one in (q_turned, o_acc, rows_turned):
                pe.sem_inc(counted_from_one, 1)

            pe.wait_ge(const_landed, 16)
            pe.wait_ge(gain_t_landed, 16)
            tensor.transpose(ps[:, 7, 0:P], gain_rows, ident[:]).then_inc(gain_t_turned, 1)
            pe.wait_ge(misc_landed, 32)
            tensor.transpose(ps[:, 3, 0:3 * KT], misc_rows, ident[0:3 * KT, 0:3 * KT]).then_inc(misc_turned, 1)
            pe.wait_ge(table_ready, 48)
            tensor.matmul(ps[0:H, 4, 0:ND], table, rows_back, start=True, stop=True).then_inc(line_acc, 1)
            for t in range(TOK):
                for c in range(NC):
                    first = S - 1 + t * P - c * CMP_STRIDE - (CMP_BLOCK - 1)
                    at = (t * NC + c) * H
                    done = tensor.matmul(ps[:, 5, at:at + H], rows_fwd[:, first:first + P], table, start=True, stop=True)
            done.then_inc(bias_cmp_acc, 1)
            pe.wait_ge(pe_rows_landed, 48)
            tensor.transpose(ps[:, 6, 0:2 * CMP_BLOCK], pe_rows, ident[0:2 * CMP_BLOCK, 0:2 * CMP_BLOCK]
                             ).then_inc(pe_turned, 1)
            pe.wait_ge(x_landed, 16 * TOK)
            pe.wait_ge(gain_t_ready, 1)
            pe.wait_ge(line_ready, 1)
            pe.wait_ge(bias_cmp_ready, 1)
            pe.wait_ge(pe_t_ready, 1)
            pe.wait_ge(lb_in, 1)

            turned_chunk(0, 0, 0, xs, lambda f: None)
            with pe.Fori(0, N_IN // 2 - 1) as i:
                for j in (1, 2):
                    wide_chunk(i * 2 + j, i * 2 + j, j % 2)
            wide_chunk(N_IN - 1, N_IN - 1, 1)

            pe.wait_ge(wg_ready, 1)
            for t in range(TOK):
                for kt in range(KT):
                    done = three_passes(ps[:, 6, t * 3 * H:(t + 1) * 3 * H], kt, t, wg_hi[:, kt, :], wg_lo[:, kt, :],
                                        kt == 0, kt == KT - 1)
            done.then_inc(gate_acc, 1)
            pe.wait_ge(acc_free, 2 + N_IN)
            for i in range(2):
                for g in range(G):
                    for t in range(TOK):
                        first = (H + (i * G) + g) * P
                        done = tensor.transpose(ps[:, 2 * i + g // 2, (g % 2) * S + t * P:(g % 2) * S + (t + 1) * P],
                                                qkv[:, t, first:first + P], ident[:])
                done.then_inc(raw_kv_turned, 1)
            for i in range(2):
                pe.wait_ge(cmp_rows_ready, i + 1)
                for j in (2 * i, 2 * i + 1):
                    pe.wait_ge(w_landed[j], 16 * (N_IN + 1))
                for l in range(CMP_BLOCK):
                    j = 2 * i + l // 16
                    done = tensor.matmul(ps[:, 4 + i, 0:G * NC], raw[:, j, (l % 16) * P:(l % 16 + 1) * P],
                                         cmp_rows[:, l].rearrange("p g c -> p (g c)"), start=l == 0,
                                         stop=l == CMP_BLOCK - 1)
                done.then_inc(cmp_done, 1)
            pe.wait_ge(gelu_ready, 1)
            tensor.matmul(ps[:, 6, 0:G * NC], w2[:, 0, :], gelu_out[:, 0], start=True, stop=True).then_inc(cmp_out, 1)
            pe.wait_ge(gelu_ready, 2)
            for g in range(G):
                done = tensor.matmul(ps[0:NC, 7, g * P:(g + 1) * P], gelu_out[:, 1, g * NC:(g + 1) * NC], w2[:, 1, :],
                                     start=True, stop=True)
            done.then_inc(cmp_out, 1)
            pe.wait_ge(cmp_ready, 2)
            with pe.Fori(0, G) as g:
                pe.wait_ge(q_staged, g + 1)
                pe.wait_ge(o_ready, g + 1)
                for h in range(R):
                    for t in range(TOK):
                        done = tensor.transpose(ps[:, 4 + h // 2, (h % 2) * S + t * P:(h % 2) * S + (t + 1) * P],
                                                staged_q[:, t, h * P:(h + 1) * P], ident[:])
                done.then_inc(q_turned, 1)
                pe.wait_ge(kv_staged, g + 1)
                for b in range(2):
                    for t in range(TOK):
                        done = tensor.transpose(ps[:, 6, b * S + t * P:b * S + (t + 1) * P], staged_kv[:, t, 2 * b, :],
                                                ident[:])
                done.then_inc(k_turned, 1)
                pe.wait_ge(q_ready, g + 1)
                for t in range(TOK):
                    for h in range(R):
                        at = (t * R + h) * NC
                        done = tensor.matmul(ps[:, 7, at:at + NC], q_t[:, h, t * P:(t + 1) * P],
                                             k_cmp[:, bass.ds(g * NC, NC)], start=True, stop=True)
                done.then_inc(cmp_logits, 1)
                pe.wait_ge(k_ready, g + 1)
                for b in range(2):
                    for h in range(R):
                        tensor.matmul(ps[:, 3 * b, h * P:(h + 1) * P], q_t[:, h, 0:P], k_t[:, b, 0:P],
                                      start=True, stop=True)
                        done = tensor.matmul(ps[:, 3 * b + 1 + h // 2, (h % 2) * S:(h % 2 + 1) * S], q_t[:, h, P:S],
                                             k_t[:, b, :], start=True, stop=True)
                    done.then_inc(logits_acc, 1)
                pe.wait_ge(p_cmp_ready, g + 1)
                for h in range(R):
                    for t in range(TOK):
                        done = tensor.transpose(ps[0:NC, 6 + h // 2, (h % 2) * S + t * P:(h % 2) * S + (t + 1) * P],
                                                p_cmp[:, t, h, :], ident[:])
                done.then_inc(p_cmp_turned, 1)
                for b in range(2):
                    pe.wait_ge(p_ready, g * 2 + (b + 1))
                    for h in range(R):
                        high = ps[:, 3 * b + h // 2, :]
                        base = (h % 2) * S
                        tensor.transpose(high[:, base:base + P], section(logits[:, b], 0, h), ident[:])
                        above = section(logits[:, b], 1, h)
                        tensor.transpose(high[:, base + P:base + S], above[:, 0:P], ident[:])
                        done = tensor.transpose(ps[:, 3 * b + 2, h * P:(h + 1) * P], above[:, P:S], ident[:])
                    done.then_inc(p_turned, 1)
                def values(b):
                    both, late = p_t_of(b)[:, 0:R * S], p_t_of(b)[:, R * S:R * S + R * P]
                    for h in range(R):
                        acc = ps[:, h // 2, (h % 2) * S:(h % 2 + 1) * S]
                        tensor.matmul(acc, staged_kv[:, 0, 2 * b + 1, :], both[:, h * S:(h + 1) * S],
                                      start=b == 0 and h % 2 == 0, stop=False, skip_group_check=True)
                        done = tensor.matmul(acc[:, P:S], staged_kv[:, 1, 2 * b + 1, :], late[:, h * P:(h + 1) * P],
                                             start=False, stop=b == 1, skip_group_check=True)
                    return done

                pe.wait_ge(p_t_ready, g * 2 + 1)
                values(0)
                pe.wait_ge(pc_t_ready, g + 1)
                for h in range(R):
                    tensor.matmul(ps[:, h // 2, (h % 2) * S:(h % 2 + 1) * S], v_cmp_now[:],
                                  pc_t[:, h * S:(h + 1) * S], start=False, stop=False, skip_group_check=True)
                pe.wait_ge(p_t_ready, g * 2 + 2)
                values(1).then_inc(o_acc, 1)
            pe.wait_ge(o_ready, G + 1)

            for c in range(N_OUT):
                wide_chunk(PR["out"] + c, WC["out"] + c, c % 2)
            mlp_layer(0, 1, 0)
            if FULL:
                gated_layer()


_INS = ["x", "norm_g", "rel_table", "nsa_w_in", "nsa_cmp_pe", "nsa_cmp_w1", "nsa_cmp_w2", "nsa_w_out", "hgrn_w_in",
        "hgrn_lb", "hgrn_onorm", "hgrn_w_out", "mlp_w_up", "mlp_w_down"]


def shape_constants(seq):
    dist = np.arange(-(seq - 1), seq)
    n = np.maximum(dist, 0)
    exact = BUCKETS // 2
    far = exact + (np.log(np.maximum(n, 1) / exact) / np.log(MAX_DIST / exact) * (BUCKETS - exact)).astype(np.int64)
    bucket = np.where(n < exact, n, np.minimum(far, BUCKETS - 1))
    rows = np.zeros((BUCKETS + 1, dist.size), np.float32)
    rows[bucket, np.arange(dist.size)] = 1.0
    rows[:, dist < 0] = 0.0
    rows[BUCKETS, dist < 0] = NEG
    pos = np.arange(seq).reshape(-1, P).T
    key, query = np.arange(P)[:, None], np.arange(P)[None, :]
    levels = []
    for j in range(LEVELS):
        m = CHUNK >> j
        pairs = (key // (2 * m) == query // (2 * m)) & (key // m % 2 == 0)
        levels.append(pairs[:, np.arange(P) // m % 2 == 1])
    return {
        "identity": np.eye(P, dtype=np.float32),
        "bucket_rows": rows,
        "bucket_rows_back": np.ascontiguousarray(rows[:, ::-1]),
        "any_cmp": (pos >= CMP_BLOCK - 1).astype(np.float32),
        "level_masks": np.stack(levels, 1).astype(np.float32),
    }


def kernel(**inputs):
    import concourse.bacc as bacc
    from concourse.bass_utils import run_bass_kernel_spmd

    nc = bacc.Bacc("TRN2", target_bir_lowering=False, num_devices=1)
    arrays, args = {}, []
    values = [(name, np.ascontiguousarray(inputs[name])) for name in _INS]
    values += list(shape_constants(inputs["x"].shape[1]).items())
    for name, a in values:
        arrays[f"in_{name}"] = a
        args.append(nc.dram_tensor(f"in_{name}", a.shape, mybir.dt.from_np(a.dtype), kind="ExternalInput").ap())
    args.append(nc.dram_tensor("out_0", inputs["x"].shape, F32, kind="ExternalOutput").ap())
    trunk_kernel(nc, *args)
    result = run_bass_kernel_spmd(nc, [arrays], core_ids=[0])
    return result.results[0]["out_0"]
```

```python
from contextlib import ExitStack

import numpy as np

import concourse.bass as bass
from concourse import mybir

ALU = mybir.AluOpType
ACT = mybir.ActivationFunctionType
AX = mybir.AxisListType
F32 = mybir.dt.float32
F32R = mybir.dt.float32r
BF16 = mybir.dt.bfloat16
U32 = mybir.dt.uint32

P = 128
EPS = 1e-6
NEG = -1.0e30
TINY = 1.0e-18
BUCKETS = 32
MAX_DIST = 128
CMP_BLOCK = 32
CMP_STRIDE = 16
LEVELS = 7
CHUNK = 64

RING = 4
SLOT = 2048
ACT_STEPS, DVE_STEPS = 8, 3
GATED_PARTS = (1, 0, 2, 3)
PIECE = 1024
SPLITS = 4
PIECES = RING * SLOT // PIECE
BANKS = (3, 0)
AHEAD = 3


def trunk_kernel(nc, x, norm_g, rel_table, nsa_w_in, nsa_cmp_pe, nsa_cmp_w1, nsa_cmp_w2, nsa_w_out,
                 hgrn_w_in, hgrn_lb, hgrn_onorm, hgrn_w_out, mlp_w_up, mlp_w_down,
                 identity, bucket_rows_back, any_cmp, level_masks, out):
    S, D = x.shape[1], x.shape[2]
    TOK = S // P
    KT = D // P
    F = mlp_w_up.shape[2]
    H = rel_table.shape[1]
    G = ((nsa_w_in.shape[2] - 3 * H) // P - H) // 6
    R = H // G
    NC = S // CMP_STRIDE - CMP_BLOCK // CMP_STRIDE + 1
    COLS = 512
    QKV = (H + 6 * G) * P
    assert TOK == 2 and KT == 16 and H == 16 and G == 4 and QKV == 5120 and NC == 15
    SCALE = float(P) ** -0.5
    LOW_NC = (P - CMP_BLOCK) // CMP_STRIDE + 1
    assert CMP_BLOCK == 2 * CMP_STRIDE and P % CMP_STRIDE == 0
    ND = 2 * S - 1

    N_IN, N_OUT, N_UP, N_GATED = QKV // COLS, D // COLS, F // COLS, 4 * D // COLS
    HALVES, DOWN_ROUNDS = 2, F // P // PIECES
    PR = {}
    n = 0
    for name, rounds in (("in", N_IN), ("out", N_OUT), ("up0", N_UP), ("down0", HALVES * DOWN_ROUNDS),
                         ("gated", N_GATED), ("out1", N_OUT), ("up1", N_UP), ("down1", HALVES * DOWN_ROUNDS)):
        PR[name] = n
        n += rounds
    WC = {}
    n = 0
    for name, chunks in (("in", N_IN), ("out", N_OUT), ("up0", N_UP), ("gated", N_GATED), ("out1", N_OUT),
                         ("up1", N_UP)):
        WC[name] = n
        n += chunks

    with ExitStack() as ctx:
        def sb(name, shape, dt=F32, stack=ctx):
            return stack.enter_context(nc.sbuf_tensor(name, shape, dt))

        def sem(name):
            return ctx.enter_context(nc.semaphore(name))

        def dram(name, shape):
            return nc.dram_tensor(name, shape, F32).ap()

        ps = ctx.enter_context(nc.psum_tensor("ps", [P, 8, COLS], F32))

        xs = sb("xs", [P, TOK, D])
        ys = sb("ys", [P, TOK, D])
        at_hi = sb("at_hi", [P, KT, S], F32R)
        at_lo = sb("at_lo", [P, KT, S], F32R)
        raw = sb("raw", [P, RING, SLOT])
        w_hi = sb("w_hi", [P, SPLITS, PIECE], F32R)
        w_lo = sb("w_lo", [P, SPLITS, PIECE], F32R)
        gain = sb("gain", [P, D])
        junk = sb("junk", [P, D // 2], BF16)
        ident = sb("ident", [P, P])
        gain_t = sb("gain_t", [P, P])
        ysq = sb("ysq", [P, TOK, N_OUT])
        ymean = sb("ymean", [P, TOK])
        yrstd = sb("yrstd", [P, TOK])
        xsq = sb("xsq", [P, TOK, 2])
        xmean = sb("xmean", [P, TOK])
        xrstd = sb("xrstd", [P, TOK])
        minus_half = sb("minus_half", [P, 8])
        relu_rows = sb("relu_rows", [P, TOK, COLS])
        misc_t = sb("misc_t", [P, 3 * KT])
        log_lb = sb("log_lb", [P, KT])
        log_rest = sb("log_rest", [P, KT])

        nsa = ExitStack()
        qkv = sb("qkv", [P, TOK, QKV], stack=nsa)
        q_t = sb("q_t", [P, R, S], stack=nsa)
        k_t = sb("k_t", [P, 2, S], stack=nsa)
        cmp_rows_v = sb("cmp_rows_v", [P, CMP_BLOCK, G, NC], stack=nsa)
        v_cmp = sb("v_cmp", [NC, G, P], stack=nsa)
        k_cmp = sb("k_cmp", [P, G * NC], stack=nsa)
        gate = sb("gate", [P, 3, TOK, H], stack=nsa)
        any_sb = sb("any_sb", [P, TOK], stack=nsa)
        stat = sb("stat", [P, 3, TOK, R], stack=nsa)
        total = sb("total", [P, 3, TOK, R], stack=nsa)
        weight = sb("weight", [P, 3, TOK, R], stack=nsa)
        p_cmp = sb("p_cmp", [P, TOK, R, NC], stack=nsa)
        early = ExitStack()
        wg_hi = sb("wg_hi", [P, KT, 3 * H], F32R, stack=early)
        wg_lo = sb("wg_lo", [P, KT, 3 * H], F32R, stack=early)
        early.close()
        v_cmp_now = sb("v_cmp_now", [NC, P], stack=nsa)
        p_t = sb("p_t", [P, 3, COLS], stack=nsa)
        nsa.close()
        gated = ExitStack()
        GT = R * S
        v_rows = sb("v_rows", [P, TOK, COLS], stack=gated)
        log_a = sb("log_a", [P, GT], stack=gated)
        log_b = sb("log_b", [P, GT], stack=gated)
        log_c = sb("log_c", [P, GT], stack=gated)
        key = sb("key", [P, GT], stack=gated)
        query = sb("query", [P, GT], stack=gated)
        run = sb("run", [P, GT], stack=gated)
        decay = sb("decay", [P, 2, GT], stack=gated)
        far_q = sb("far_q", [P, 2, GT // 2], stack=gated)
        mix_t = sb("mix_t", [P, R * TOK, P], stack=gated)
        cross_t = sb("cross_t", [P, R, P], stack=gated)
        gate_rows = sb("gate_rows", [P, TOK, COLS], stack=gated)
        restart = sb("restart", [P, GT], stack=gated)
        masks = sb("masks", [P, LEVELS, P // 2], stack=gated)
        lb_now = sb("lb_now", [P, R], stack=gated)
        rest_now = sb("rest_now", [P, R], stack=gated)
        last_sum = sb("last_sum", [P, R], stack=gated)
        osq = sb("osq", [P, TOK * R], stack=gated)
        orstd = sb("orstd", [P, TOK * R], stack=gated)
        gated.close()

        ys_flat = ys[:].rearrange("p t d -> p (t d)")
        logits = ys_flat[:, 0:6 * COLS].rearrange("p (b n c) -> p b n c", b=2, n=3)
        bias = ys_flat[:, 6 * COLS:8 * COLS].rearrange("p (h k) -> p h k", h=R)
        line_rows = ys_flat[:, 6 * COLS:7 * COLS]
        kv0 = H * P
        staged_q = qkv[:, :, kv0:kv0 + R * P]
        staged_kv = qkv[:, :, kv0 + G * P:kv0 + 2 * G * P].rearrange("p t (s d) -> p t s d", s=4)
        cmp_rows = (ys_flat[:, 0:CMP_BLOCK * G * NC].rearrange("p (l g c) -> p l g c", l=CMP_BLOCK, g=G), cmp_rows_v[:])
        rows_flat = relu_rows[:].rearrange("p t c -> p (t c)")
        wg_raw = rows_flat[:, 0:KT * 3 * H].rearrange("p (k n) -> p k n", k=KT)
        gain_rows = rows_flat[:, KT * 3 * H:KT * 3 * H + P]
        misc_rows = rows_flat[0:3 * KT, KT * 3 * H + P:KT * 3 * H + 2 * P]
        pc_t = rows_flat[0:NC, 0:R * S]
        p_cmp_flat = p_cmp[:].rearrange("p t h c -> p (t h c)")
        at = [0]

        def small(rows, cols):
            at[0] += cols
            return gain[0:rows, at[0] - cols:at[0]]

        rows_back = small(BUCKETS + 1, ND)
        gate_t = gain[0:3 * H, 0:S]
        table = small(BUCKETS + 1, H)
        pe_rows = small(2 * CMP_BLOCK, P)
        w2 = small(P, 2 * P).rearrange("p (i n) -> p i n", i=2)
        pe_t = small(P, 2 * CMP_BLOCK)
        gelu_z, gelu_u, gelu_e = (small(G * NC, P) for _ in range(3))
        gelu_out = small(G * NC, 2 * P).rearrange("p (i n) -> p i n", i=2)
        gelu_t = small(P, 2 * G * NC).rearrange("p (i n) -> p i n", i=2)
        lb_tmp = small(P, 6 * KT).rearrange("p (i k) -> p i k", i=6)
        gate_tmp = small(P, TOK * 3 * H).rearrange("p (t n) -> p t n", t=TOK)

        def section(rows, t, h):
            return rows[:, 0, h * P:(h + 1) * P] if t == 0 else rows[:, 1 + h // 2, (h % 2) * S:(h % 2 + 1) * S]

        def section0(rows):
            return rows[:, 0, :].rearrange("p (h k) -> p h k", h=R)

        def p_t_of(b):
            return p_t[:].rearrange("p n c -> p (n c)") if b == 0 else logits[:, 0].rearrange("p n c -> p (n c)")

        mlp = ExitStack()
        hidden_t = sb("hidden_t", [P, F // P, S], stack=mlp)
        mlp.close()

        w_landed = [sem(f"w_landed{j}") for j in range(RING)]
        hi_ready = sem("hi_ready")
        lo_ready = sem("lo_ready")
        split_free = sem("split_free")
        acc_free = sem("acc_free")
        x_landed = sem("x_landed")
        rows_landed = sem("rows_landed")
        gain_landed = sem("gain_landed")
        vectors_turned = sem("vectors_turned")
        gain_t_ready = sem("gain_t_ready")
        half_ready = sem("half_ready")
        x_ready = sem("x_ready")
        xt_ready = sem("xt_ready")
        at_hi_ready = sem("at_hi_ready")
        at_ready = sem("at_ready")
        xsq_ready = sem("xsq_ready")
        xmean_ready = sem("xmean_ready")
        xrstd_ready = sem("xrstd_ready")
        ysq_ready = sem("ysq_ready")
        y_seq = sem("y_seq")
        ymean_ready = sem("ymean_ready")
        yrstd_ready = sem("yrstd_ready")
        rows_turned = sem("rows_turned")
        hidden_ready = sem("hidden_ready")
        stored = sem("stored")
        wg_landed = sem("wg_landed")
        wg_hi_ready = sem("wg_hi_ready")
        wg_ready = sem("wg_ready")
        gate_acc = sem("gate_acc")
        gate_t_ready = sem("gate_t_ready")
        gate_turned = sem("gate_turned")
        gate_raw = sem("gate_raw")
        gate_exp = sem("gate_exp")
        table_landed = sem("table_landed")
        table_ready = sem("table_ready")
        line_acc = sem("line_acc")
        line_ready = sem("line_ready")
        line_stored = sem("line_stored")
        square_stored = sem("square_stored")
        w2_landed = sem("w2_landed")
        pe_t_ready = sem("pe_t_ready")
        raw_kv_turned = sem("raw_kv_turned")
        cmp_rows_ready = sem("cmp_rows_ready")
        cmp_done = sem("cmp_done")
        gelu_exp = sem("gelu_exp")
        gelu_in = sem("gelu_in")
        gelu_ready = sem("gelu_ready")
        gelu_turned = sem("gelu_turned")
        gelu_t_ready = sem("gelu_t_ready")
        cmp_out = sem("cmp_out")
        cmp_ready = sem("cmp_ready")
        small_seq = sem("small_seq")
        bias_landed = sem("bias_landed")
        q_staged = sem("q_staged")
        k_staged = sem("k_staged")
        v_staged = sem("v_staged")
        q_turned = sem("q_turned")
        k_turned = sem("k_turned")
        q_ready = sem("q_ready")
        k_ready = sem("k_ready")
        cmp_logits = sem("cmp_logits")
        logits_acc = sem("logits_acc")
        cmp_max = sem("cmp_max")
        max_ready = sem("max_ready")
        cmp_exp = sem("cmp_exp")
        exp_ready = sem("exp_ready")
        p_cmp_ready = sem("p_cmp_ready")
        p_ready = sem("p_ready")
        p_cmp_turned = sem("p_cmp_turned")
        p_turned = sem("p_turned")
        pc_t_ready = sem("pc_t_ready")
        p_t_ready = sem("p_t_ready")
        o_acc = sem("o_acc")
        o_hi_ready = sem("o_hi_ready")
        o_ready = sem("o_ready")
        grp_seq = sem("grp_seq")

        misc_t_ready = sem("misc_t_ready")
        lb_in = sem("lb_in")
        lb_out = sem("lb_out")
        lb_ready = sem("lb_ready")
        masks_landed = sem("masks_landed")
        dve_waited = sem("dve_waited")
        pool_waited = sem("pool_waited")
        act_seq = sem("act_seq")
        dve_seq = sem("dve_seq")
        f_turned = sem("f_turned")
        f_log = sem("f_log")
        f_read = sem("f_read")
        odds_ready = sem("odds_ready")
        key_ready = sem("key_ready")
        odds_log = sem("odds_log")
        q_turned1 = sem("q_turned1")
        q_log = sem("q_log")
        q_min = sem("q_min")
        q_sigmoid = sem("q_sigmoid")
        query_ready = sem("query_ready")
        diag_acc = sem("diag_acc")
        diag_read = sem("diag_read")
        delta_ready = sem("delta_ready")
        decay_ready = sem("decay_ready")
        sides_ready = sem("sides_ready")
        level_acc = sem("level_acc")
        level_read = sem("level_read")
        run_ready = sem("run_ready")
        last_sum_ready = sem("last_sum_ready")
        gate_log = sem("gate_log")
        gate_min = sem("gate_min")
        gate_sigmoid = sem("gate_sigmoid")
        mix_acc = sem("mix_acc")
        osq_ready = sem("osq_ready")
        omean_ready = sem("omean_ready")
        orstd_ready = sem("orstd_ready")
        mix_ready = sem("mix_ready")

        class Steps:

            def __init__(self, engine, semaphore):
                self.engine, self.semaphore, self.before, self.base, self.n = engine, semaphore, 0, 0, 0

            def turn(self, i, per):
                if self.n:
                    self.before += self.n
                self.base, self.n = self.before + i * per, 0

            def leave(self, turns, per):
                assert self.n == per, (self.n, per)
                self.before += turns * per
                self.base, self.n = self.before, 0

            def link(self, done):
                self.n += 1
                done.then_inc(self.semaphore, 1)
                self.engine.wait_ge(self.semaphore, self.base + self.n)
                return done

        x_rows = x.rearrange("b (t p) d -> p (b t) d", p=P)
        out_rows = out.rearrange("b (t p) d -> p (b t) d", p=P)
        bias_line = dram("bias_line", (H, ND))
        bias_square = dram("bias_square", (H, P, S))

        def by_feature(w):
            return w.rearrange("(k p) n -> p k n", p=P)

        w_in, w_out = by_feature(nsa_w_in[0]), by_feature(nsa_w_out[0])
        w_gated, w_out1 = by_feature(hgrn_w_in[0]), by_feature(hgrn_w_out[0])
        w_up = [by_feature(mlp_w_up[i]) for i in range(2)]
        w_down = [by_feature(mlp_w_down[i]) for i in range(2)]

        PAIR = ((0, 0), (0, 1), (1, 0), (1, 1), (0, 2), (1, 2), (0, 3), (1, 3))
        FILL_TURNED = (28, 29, 30, 31, 33, 34)
        FILL_SPLIT = (32, 33, 34, 35, 37, 38, 32 + 15, 32 + 15)
        LATE_FILLS, LATE_TURNED = (6, 7), 12

        def tail_steps(q):
            return range(32 + (3 * q + 1) // 2, 32 + (3 * q + 4) // 2)

        def chunk_done(pr):
            return PIECES * pr + (PIECES + SPLITS)

        def halves(a, m):
            blocks = a.rearrange("p (n two m) -> p n two m", two=2, m=m)
            return blocks[:, :, 0, :], blocks[:, :, 1, :]

        block = ctx.enter_context(nc.Block())

        @block.sync
        def _(sp):
            def wait_slot(j, pr):
                sp.wait_ge(lo_ready, PIECES * pr + (2 * j + 2 - PIECES))

            def load_wide(w, chunk, pr, ring_is_free=False):
                for j in range(RING):
                    if not ring_is_free:
                        wait_slot(j, pr)
                    sp.dma_start(raw[:, j, :].rearrange("p (k n) -> p k n", k=4),
                                 w[:, 4 * j:4 * j + 4, bass.ds(chunk * COLS, COLS)]).then_inc(w_landed[j], 16)

            def load_down(w, half, rnd, pr):
                cols = slice(half * 2 * COLS, (half + 1) * 2 * COLS)
                for j in range(RING):
                    wait_slot(j, pr)
                    sp.dma_start(raw[:, j, :].rearrange("p (k n) -> p k n", k=2),
                                 w[:, bass.ds(rnd * PIECES + 2 * j, 2), cols]).then_inc(w_landed[j], 16)

            def load_mlp(layer):
                with sp.Fori(0, N_UP) as i:
                    load_wide(w_up[layer], i, i + PR[f"up{layer}"])
                for half in range(HALVES):
                    with sp.Fori(0, DOWN_ROUNDS) as i:
                        load_down(w_down[layer], half, i, i + (PR[f"down{layer}"] + half * DOWN_ROUNDS))

            for t in range(TOK):
                sp.dma_start(xs[:, t, :], x_rows[:, t, :]).then_inc(x_landed, 16)
            load_wide(w_in, 0, 0, ring_is_free=True)
            with sp.Fori(1, N_IN) as i:
                load_wide(w_in, i, i)
            for j in range(RING):
                wait_slot(j, N_IN)
                w1 = nsa_cmp_w1[0, j // 2].rearrange("(l d) n -> d l n", d=P)
                sp.dma_start(raw[:, j, :].rearrange("p (l n) -> p l n", l=16),
                             w1[:, 16 * (j % 2):16 * (j % 2) + 16, :]).then_inc(w_landed[j], 16)
            sp.wait_ge(cmp_done, 2)
            load_wide(w_out, 0, PR["out"], ring_is_free=True)
            with sp.Fori(1, N_OUT) as i:
                load_wide(w_out, i, i + PR["out"])
            load_mlp(0)
            with sp.Fori(0, G) as g:
                for kind, part in enumerate(GATED_PARTS):
                    load_wide(w_gated, g + part * N_OUT, g * 4 + (PR["gated"] + kind))
            for n, (c, quarter) in enumerate(PAIR):
                j = n % RING
                wait_slot(j, PR["out1"] + n // RING)
                sp.dma_start(raw[:, j, :].rearrange("p (k n) -> p k n", k=4),
                             w_out1[:, 4 * quarter:4 * quarter + 4, c * COLS:(c + 1) * COLS]
                             ).then_inc(w_landed[j], 16)
            with sp.Fori(2, N_OUT) as i:
                load_wide(w_out1, i, i + PR["out1"])
            load_mlp(1)
            last = 3
            for n in range(N_OUT):
                sp.wait_ge(x_ready, N_OUT * last + n + 1)
                cols = slice(n * COLS, (n + 1) * COLS)
                sp.dma_start(out_rows[:, :, cols], xs[:, :, cols]).then_inc(stored, 16)
            sp.wait_ge(stored, 16 * N_OUT)

        @block.gpsimd
        def _(pool):
            def load_gain(layer, norm):
                pool.dma_start(gain[:], bass.AP(norm_g.tensor, (layer * 4 + norm) * D, [[0, P], [1, D]])
                               ).then_inc(gain_landed, 16)

            def x_factor(k):
                pool.wait_ge(xsq_ready, 2 * TOK * (k + 1))
                nc.gpsimd.tensor_tensor(xmean[:], xsq[:, :, 0], xsq[:, :, 1], ALU.add).then_inc(xmean_ready, 1)
                pool.wait_ge(xmean_ready, 2 * k + 1)
                nc.gpsimd.tensor_scalar(xmean[:], xmean[:], 1.0 / D, EPS, ALU.mult, ALU.add).then_inc(xmean_ready, 1)
                pool.wait_ge(xmean_ready, 2 * k + 2)
                nc.gpsimd.tensor_tensor(xrstd[:], xmean[:], minus_half[:, 0:TOK], ALU.pow).then_inc(xrstd_ready, 1)

            def y_factor(u):
                pool.wait_ge(ymean_ready, u + 1)
                nc.gpsimd.tensor_tensor(yrstd[:], ymean[:], minus_half[:, 0:TOK], ALU.pow).then_inc(yrstd_ready, 1)

            def wait_and_carry(semaphore, value):
                pool.wait_ge(semaphore, value)
                pool.sem_inc(pool_waited, 1)

            def delta(j, g):
                if j >= 2:
                    wait_and_carry(level_acc, g * (LEVELS + 1) + (j - 1))
                to = decay[:, j % 2]
                if j < LEVELS:
                    m = CHUNK >> j
                    (first, second), (to_first, to_second) = halves(run[:], m), halves(to, m)
                    ends = first[:, :, m - 1:m].broadcast_to((P, GT // (2 * m), m))
                    nc.gpsimd.tensor_tensor(to_first, ends, first, ALU.subtract)
                    if m == CHUNK:
                        done = nc.gpsimd.tensor_copy(to_second, second)
                    else:
                        done = nc.gpsimd.tensor_tensor(to_second, second, ends, ALU.subtract)
                else:
                    chunks = run[:].rearrange("p (h c m) -> p h c m", c=4, m=CHUNK)
                    out_chunks = to.rearrange("p (h c m) -> p h c m", c=4, m=CHUNK)

                    def end(c):
                        return chunks[:, :, c, CHUNK - 1:CHUNK].broadcast_to((P, R, CHUNK))

                    nc.gpsimd.tensor_tensor(last_sum[:], chunks[:, :, 0, CHUNK - 1], chunks[:, :, 1, CHUNK - 1],
                                            ALU.add).then_inc(last_sum_ready, 1)
                    wait_and_carry(last_sum_ready, g + 1)
                    nc.gpsimd.tensor_tensor(out_chunks[:, :, 0], last_sum[:].unsqueeze(2).broadcast_to((P, R, CHUNK)),
                                         chunks[:, :, 0], ALU.subtract)
                    nc.gpsimd.tensor_tensor(out_chunks[:, :, 1], end(1), chunks[:, :, 1], ALU.subtract)
                    nc.gpsimd.tensor_copy(out_chunks[:, :, 2], chunks[:, :, 2])
                    done = nc.gpsimd.tensor_tensor(out_chunks[:, :, 3], chunks[:, :, 3], end(2), ALU.add)
                done.then_inc(delta_ready, 1)

            pool.sem_inc(orstd_ready, 1)
            nc.gpsimd.memset(minus_half[:], -0.5).then_inc(half_ready, 1)
            pool.wait_ge(half_ready, 1)
            nc.gpsimd.memset(table, 1.0).then_inc(table_landed, 1)
            pool.wait_ge(table_landed, 1)
            pool.dma_start(table[0:BUCKETS, :], rel_table).then_inc(table_ready, 16)
            pool.dma_start(rows_back, bucket_rows_back).then_inc(table_ready, 16)
            x_factor(0)
            pool.dma_start(w2, nsa_cmp_w2[0].rearrange("i k n -> k i n")).then_inc(w2_landed, 16)
            pool.dma_start(any_sb[:], any_cmp).then_inc(w2_landed, 16)
            pool.dma_start(wg_raw, w_in[:, :, QKV:QKV + 3 * H]).then_inc(wg_landed, 16)
            pool.wait_ge(line_ready, 1)
            pool.dma_start(bias_line, line_rows[0:H, 0:ND]).then_inc(line_stored, 16)
            pool.wait_ge(line_stored, 16)
            pool.dma_start(bias_square, bass.AP(bias_line.tensor, P - 1, [[ND, H], [-1, P], [1, S]])
                           ).then_inc(square_stored, 16)
            pool.wait_ge(square_stored, 16)
            with pool.Fori(0, G) as g:
                pool.wait_ge(max_ready, 2 * g + 1)
                pool.dma_start(bias, bias_square[bass.ds(g * R, R)].rearrange("h p k -> p h k")
                               ).then_inc(bias_landed, 16)
            pool.wait_ge(cmp_ready, 2)
            load_gain(0, 1)
            y_factor(0)
            x_factor(1)
            pool.wait_ge(x_ready, N_OUT)
            load_gain(0, 3)
            y_factor(1)
            pool.wait_ge(x_ready, 2 * N_OUT)
            pool.dma_start(masks[:], level_masks).then_inc(masks_landed, 16)
            load_gain(1, 1)
            x_factor(2)
            with pool.Fori(0, G) as g:
                wait_and_carry(run_ready, g + 1)
                for j in range(LEVELS + 1):
                    delta(j, g)
                wait_and_carry(osq_ready, g + 1)
                nc.gpsimd.tensor_scalar(osq[:], osq[:], 1.0 / P, EPS, ALU.mult, ALU.add).then_inc(omean_ready, 1)
                pool.wait_ge(omean_ready, g + 1)
                nc.gpsimd.tensor_tensor(orstd[:], osq[:], minus_half[:], ALU.pow).then_inc(orstd_ready, 1)
            y_factor(2)
            x_factor(3)
            pool.wait_ge(x_ready, 3 * N_OUT)
            load_gain(1, 3)
            y_factor(3)

        @block.scalar
        def _(act):
            scalar = nc.scalar
            junk_user = []

            def own_junk():
                if junk_user:
                    act.wait_ge(*junk_user[-1])

            def split_hi(p, pr, rr):
                j = p // 2
                if p % 2 == 0:
                    act.wait_ge(w_landed[j], 16 * rr + 16)
                act.wait_ge(split_free, PIECES * pr + (p + 1))
                scalar.copy(w_hi[:, p % SPLITS, :], raw[:, j, (p % 2) * PIECE:(p % 2 + 1) * PIECE]
                            ).then_inc(hi_ready, 1)

            def wide_chunk(pr, rr, between, around=lambda p: None):
                for p in range(PIECES):
                    if p != AHEAD:
                        around(p)
                    else:
                        between()
                    split_hi(p, pr, rr)

            def down_round(half, rnd, pr, between):
                for p in range(PIECES):
                    if p == AHEAD:
                        between()
                    if p % 2 == 0:
                        act.wait_ge(w_landed[p // 2], 16 * pr + 32)
                    act.wait_ge(split_free, PIECES * pr + (p + 1))
                    scalar.copy(at_hi[:, p:p + 1, :], hidden_t[:, bass.ds(rnd * PIECES + p, 1), :])
                    scalar.copy(w_hi[:, p % SPLITS, :], raw[:, p // 2, (p % 2) * PIECE:(p % 2 + 1) * PIECE]
                                ).then_inc(hi_ready, 1)

            def turn_in(b, columns, fills=range(KT // 2), banks=4):
                for f in fills:
                    act.wait_ge(xt_ready, 8 * b + f + 1)
                    for k in range(2):
                        done = scalar.activation(at_hi[:, 2 * f + k, :], ps[:, 4 + f % banks, k * S:(k + 1) * S],
                                                 ACT.Copy, scale=columns[:, 2 * f + k:2 * f + k + 1])
                    done.then_inc(at_hi_ready, 1)

            def square_of_x(k, n):
                if k:
                    act.wait_ge(x_ready, N_OUT * k)
                else:
                    act.wait_ge(x_landed, 16 * TOK)
                own_junk()
                scalar.activation(junk[:], xs[:, n // 2, (n % 2) * D // 2:(n % 2 + 1) * D // 2], ACT.Square,
                                  accum_out=xsq[:, n // 2, n % 2:n % 2 + 1]).then_inc(xsq_ready, 1)
                junk_user.append((xsq_ready, 2 * TOK * k + n + 1))

            def squares_after(k):
                return lambda p: square_of_x(k, p - AHEAD - 1) if p > AHEAD else None

            def squares_of_y(u, n, banks, pr, pieces_after=0):
                act.wait_ge(split_free, chunk_done(pr) - pieces_after)
                for t in range(TOK):
                    own_junk()
                    scalar.activation(junk[:, 0:COLS], ps[:, banks[t], :], ACT.Square,
                                      accum_out=ysq[:, t, n:n + 1]).then_inc(ysq_ready, 1)
                    junk_user.append((ysq_ready, 2 * N_OUT * u + 2 * n + t + 1))

            def square_hidden(u, chunk):
                act.wait_ge(rows_turned, u + 2)
                scalar.activation(hidden_t[:, bass.ds(chunk * 4, 4), :].rearrange("p k s -> p (k s)"),
                                  ps[:, 4:6, :].rearrange("p b c -> p (b c)"), ACT.Square).then_inc(hidden_ready, 1)

            def wide_rows_out(name, u):
                for c in range(N_OUT):
                    pr = PR[name] + c
                    wide_chunk(pr, pr + 1, lambda: squares_of_y(u, c - 1, [2 * ((c - 1) % 2), 2 * ((c - 1) % 2) + 1],
                                                                pr - 1) if c else None)

            def mlp_layer(layer, boundary):
                up, down = PR[f"up{layer}"], PR[f"down{layer}"]
                u0 = layer * N_UP

                def up_chunk(c, between_piece):
                    for p in range(PIECES):
                        if between_piece is boundary:
                            if p == AHEAD:
                                boundary()
                            squares_after(2 * layer + 1)(p)
                        if p == AHEAD + 3 and between_piece is not boundary:
                            between_piece()
                        split_hi(p, c + up, c + (up + 1))

                up_chunk(0, boundary)
                with act.Fori(0, N_UP // 2 - 1) as i:
                    for k in (1, 2):
                        up_chunk(i * 2 + k, lambda: square_hidden(i * 2 + (u0 + k - 1), i * 2 + (k - 1)))
                up_chunk(N_UP - 1, lambda: square_hidden(u0 + N_UP - 2, N_UP - 2))
                act.wait_ge(hidden_ready, u0 + N_UP)
                u = 2 * layer + 1

                def last_hidden():
                    square_hidden(u0 + N_UP - 1, N_UP - 1)
                    act.wait_ge(hidden_ready, u0 + N_UP + 1)

                down_round(0, 0, down, last_hidden)
                with act.Fori(1, DOWN_ROUNDS) as i:
                    down_round(0, i, i + down, lambda: None)
                pr = down + DOWN_ROUNDS

                def first_half():
                    for n in range(2):
                        squares_of_y(u, n, [2 * n, 2 * n + 1], pr - 1)

                down_round(1, 0, pr, first_half)
                with act.Fori(1, DOWN_ROUNDS) as i:
                    down_round(1, i, i + pr, lambda: None)

            def second_half(u, pr):
                for n in range(2):
                    squares_of_y(u, 2 + n, [4 + 2 * n, 5 + 2 * n], pr)

            def gains(layer, norm):
                return gain_t[:, (layer * 4 + norm) * KT:(layer * 4 + norm + 1) * KT]

            def turn_x(b, layer, norm):
                turn_in(b, gains(layer, norm))

            own = Steps(act, act_seq)

            def step(t, g):
                turned = ps[:, 4:6, :].rearrange("p b c -> p (b c)")
                if t == 13:
                    act.wait_ge(f_turned, g + 1)
                    own.link(scalar.activation(log_a[:], turned, ACT.Abs))
                if t == 14:
                    own.link(scalar.activation(log_a[:], log_a[:], ACT.Exp, scale=-1.0))
                if t == 15:
                    scalar.activation(log_a[:], log_a[:], ACT.Ln, bias=1.0).then_inc(f_log, 1)
                if t == 19:
                    act.wait_ge(f_read, g + 1)
                    for h in range(R):
                        done = scalar.activation(key[:, h * S:(h + 1) * S], log_c[:, h * S:(h + 1) * S], ACT.Exp,
                                                 scale=-1.0, bias=rest_now[:, h:h + 1])
                    done.then_inc(key_ready, 1)
                if t == 20:
                    act.wait_ge(odds_ready, g + 1)
                    own.link(scalar.activation(log_a[:], log_a[:], ACT.Abs))
                if t == 21:
                    own.link(scalar.activation(log_a[:], log_a[:], ACT.Exp, scale=-1.0))
                if t == 22:
                    scalar.activation(log_a[:], log_a[:], ACT.Ln, bias=1.0).then_inc(odds_log, 1)
                if t == 23:
                    act.wait_ge(key_ready, g + 1)
                    act.wait_ge(q_turned1, g + 1)
                    own.link(scalar.activation(log_c[:], turned, ACT.Abs))
                if t == 24:
                    own.link(scalar.activation(log_c[:], log_c[:], ACT.Exp, scale=-1.0))
                if t == 25:
                    scalar.activation(log_c[:], log_c[:], ACT.Ln, bias=1.0).then_inc(q_log, 1)
                if t == 27:
                    act.wait_ge(q_min, g + 1)
                    scalar.activation(log_c[:], log_c[:], ACT.Exp).then_inc(q_sigmoid, 1)
                if 29 <= t <= 29 + 2 * LEVELS and t % 2 == 1:
                    j = (t - 29) // 2
                    act.wait_ge(delta_ready, g * (LEVELS + 1) + (j + 1))
                    scalar.activation(decay[:, j % 2], decay[:, j % 2], ACT.Exp).then_inc(decay_ready, 1)
                if t == 37:
                    act.wait_ge(acc_free, g * 4 + (WC["gated"] + 3 + 3))
                    own.link(scalar.activation(gate_rows[:], relu_rows[:], ACT.Abs))
                if t == 38:
                    own.link(scalar.activation(gate_rows[:], gate_rows[:], ACT.Exp, scale=-1.0))
                if t == 39:
                    scalar.activation(gate_rows[:], gate_rows[:], ACT.Ln, bias=1.0).then_inc(gate_log, 1)
                if t == 41:
                    act.wait_ge(gate_min, g + 1)
                    scalar.activation(gate_rows[:], gate_rows[:], ACT.Exp).then_inc(gate_sigmoid, 1)
                if t == 49:
                    act.wait_ge(mix_acc, g + 1)
                    act.wait_ge(orstd_ready, g + 1)
                    own_junk()
                    for n in range(TOK * R):
                        done = scalar.activation(junk[:, n % 8 * P:(n % 8 + 1) * P],
                                                 ps[:, 6 + n // R, (n % R) * P:(n % R + 1) * P], ACT.Square,
                                                 accum_out=osq[:, n:n + 1])
                    done.then_inc(osq_ready, 1)

            def gated_layer():
                pr = PR["gated"]
                second_half_pr = PR["down0"] + HALVES * DOWN_ROUNDS - 1

                def into_gated():
                    second_half(1, second_half_pr)
                    turn_x(2, 1, 0)

                def parts(g, before):
                    for c in range(4):
                        for p in range(PIECES):
                            t = 8 * c + p
                            if t == AHEAD and before is into_gated:
                                before()
                            if c == 0 and before is into_gated:
                                squares_after(2)(p)
                            step(t, g)
                            if before is not into_gated:
                                step(t + 32, before)
                            split_hi(p, g * 4 + (pr + c), g * 4 + (pr + c + 1))

                act.wait_ge(lb_ready, 1)
                parts(0, into_gated)
                with act.Fori(1, G - 1) as g:
                    own.turn(g - 1, ACT_STEPS)
                    parts(g, g - 1)
                own.leave(G - 2, ACT_STEPS)
                parts(G - 1, G - 2)

                pr = PR["out1"]
                for q in range(2 * PIECES):
                    for f in range(KT // 2):
                        if FILL_SPLIT[f] == 32 + q:
                            turn_in(3, misc_t[:, 2 * KT:3 * KT], (f,), 2)
                    for t in tail_steps(q):
                        step(t, G - 1)
                    split_hi(q % PIECES, pr + q // PIECES, pr + q // PIECES + 1)
                junk_user.append((osq_ready, G))
                wide_chunk(pr + 2, pr + 3, lambda: squares_of_y(2, 1, [2, 3], pr + 1),
                           lambda p: squares_of_y(2, 0, [0, 1], pr + 1, 2) if p == 1 else None)
                wide_chunk(pr + 3, pr + 4, lambda: squares_of_y(2, 2, [0, 1], pr + 2))

                def into_mlp1():
                    squares_of_y(2, N_OUT - 1, [2, 3], PR["out1"] + N_OUT - 1)
                    turn_x(4, 1, 2)

                mlp_layer(1, into_mlp1)
                second_half(3, PR["down1"] + HALVES * DOWN_ROUNDS - 1)

            def start_in():
                act.wait_ge(gain_t_ready, 1)
                turn_in(0, gains(0, 0))

            act.sem_inc(hidden_ready, 1)
            act.dma_start(ident[:], identity).then_inc(rows_landed, 16)
            act.dma_start(gain_rows, norm_g.rearrange("l n (k p) -> (l n k) p", p=P)).then_inc(rows_landed, 16)
            act.dma_start(misc_rows[0:2 * KT, :], hgrn_lb.rearrange("l (k p) -> (l k) p", p=P)).then_inc(rows_landed, 16)
            act.dma_start(misc_rows[2 * KT:3 * KT, :], hgrn_onorm[0].rearrange("(k p) -> k p", p=P)
                          ).then_inc(rows_landed, 16)
            act.dma_start(pe_rows, nsa_cmp_pe[0].rearrange("i l d -> (i l) d")).then_inc(rows_landed, 16)
            wide_chunk(0, 0, start_in, squares_after(0))
            act.wait_ge(lb_in, 1)
            scalar.activation(lb_tmp[:, 1:3], lb_tmp[:, 1:3], ACT.Exp).then_inc(lb_out, 1)
            act.wait_ge(lb_in, 2)
            scalar.activation(lb_tmp[:, 2:4], lb_tmp[:, 2:4], ACT.Ln).then_inc(lb_out, 1)
            with act.Fori(1, N_IN) as i:
                wide_chunk(i, i, lambda: None)

            def attention():
                act.wait_ge(wg_landed, 16)
                scalar.copy(wg_hi[:].rearrange("p k n -> p (k n)"), wg_raw.rearrange("p k n -> p (k n)")
                            ).then_inc(wg_hi_ready, 1)
                act.wait_ge(gate_raw, 1)
                scalar.activation(gate_tmp, gate_tmp, ACT.Exp, scale=-1.0).then_inc(gate_exp, 1)
                for i in range(2):
                    act.wait_ge(gelu_in, i + 1)
                    scalar.activation(gelu_e, gelu_u, ACT.Exp, scale=-2.0 * float(np.sqrt(2.0 / np.pi))
                                      ).then_inc(gelu_exp, 1)
                act.wait_ge(cmp_rows_ready, 2)
                act.wait_ge(raw_kv_turned, 2)

                def stage_q(g):
                    scalar.copy(staged_q, qkv[:, :, bass.ds(g * R * P, R * P)]).then_inc(q_staged, 1)

                def take_q(turns):
                    act.wait_ge(q_turned, turns)
                    scalar.activation(q_t[:].rearrange("p h s -> p (h s)"),
                                      ps[:, 4:6, :].rearrange("p b c -> p (b c)"), ACT.Copy, scale=SCALE
                                      ).then_inc(q_ready, 1)

                def group(g, last):
                    if not last:
                        stage_q(g + 1)
                    for b in range(2):
                        if b == 1:
                            act.wait_ge(cmp_max, g + 1)
                            scalar.activation(p_cmp_flat, p_cmp_flat, ACT.Exp).then_inc(cmp_exp, 1)
                        act.wait_ge(max_ready, g * 2 + (b + 1) + 1)
                        for t in range(TOK):
                            for h in range(R):
                                row = section(logits[:, b], t, h)
                                done = scalar.activation(row, row, ACT.Exp, bias=stat[:, b, t, h:h + 1],
                                                         accum_out=total[:, b, t, h:h + 1])
                        done.then_inc(exp_ready, 1)
                    act.wait_ge(p_cmp_turned, g + 1)
                    scalar.copy(pc_t, ps[0:NC, 6:8, :].rearrange("p b c -> p (b c)")).then_inc(pc_t_ready, 1)
                    for b in range(2):
                        act.wait_ge(p_turned, g * 2 + (b + 1))
                        scalar.copy(p_t_of(b), ps[:, BANKS[b]:BANKS[b] + 3, :].rearrange("p b c -> p (b c)")
                                    ).then_inc(p_t_ready, 1)
                    if not last:
                        take_q(g + 2)
                    act.wait_ge(o_acc, g + 2)
                    scalar.copy(at_hi[:, bass.ds(g * R, R), :].rearrange("p k s -> p (k s)"),
                                ps[:, 6:8, :].rearrange("p b c -> p (b c)")).then_inc(o_hi_ready, 1)

                stage_q(0)
                take_q(1)
                with act.Fori(0, G - 1) as g:
                    group(g, False)
                group(G - 1, True)

            attention()
            wide_rows_out("out", 0)
            pr = PR["out"] + N_OUT - 1

            def into_mlp0():
                squares_of_y(0, N_OUT - 1, [2, 3], pr)
                turn_x(1, 0, 2)

            mlp_layer(0, into_mlp0)
            gated_layer()

        @block.vector
        def _(dve):
            vector = nc.vector
            seq = [0]

            def chain(done):
                seq[0] += 1
                done.then_inc(small_seq, 1)
                dve.wait_ge(small_seq, seq[0])

            def split_lo(p, pr):
                dve.wait_ge(hi_ready, PIECES * pr + (p + 1))
                vector.tensor_tensor(w_lo[:, p % SPLITS, :], raw[:, p // 2, (p % 2) * PIECE:(p % 2 + 1) * PIECE],
                                     w_hi[:, p % SPLITS, :].bitcast(F32), ALU.subtract).then_inc(lo_ready, 1)

            def wide_chunk(pr, between, early=lambda p: None):
                for p in range(PIECES):
                    if p < AHEAD:
                        early(p)
                    if p == AHEAD:
                        between()
                    split_lo(p, pr)

            def down_round(rnd, pr, between):
                for p in range(PIECES):
                    if p == AHEAD:
                        between()
                    dve.wait_ge(hi_ready, PIECES * pr + (p + 1))
                    vector.tensor_tensor(at_lo[:, p, :], hidden_t[:, bass.ds(rnd * PIECES + p, 1), :].rearrange(
                        "p k s -> p (k s)"), at_hi[:, p, :].bitcast(F32), ALU.subtract)
                    vector.tensor_tensor(w_lo[:, p % SPLITS, :],
                                         raw[:, p // 2, (p % 2) * PIECE:(p % 2 + 1) * PIECE],
                                         w_hi[:, p % SPLITS, :].bitcast(F32), ALU.subtract).then_inc(lo_ready, 1)

            def y_rows(u, n, banks, pr, wide):
                cols = slice(n * COLS, (n + 1) * COLS)
                dve.wait_ge(gain_landed, 16 * (u + 1))
                for t in range(TOK):
                    dve.wait_ge(ysq_ready, 2 * N_OUT * u + 2 * n + t + 1)
                    done = vector.tensor_tensor(ys[:, t, cols], ps[:, banks[t], :], gain[:, cols], ALU.mult)
                    if wide and t == TOK - 1:
                        done.then_inc(acc_free, 1)
                    else:
                        done.then_inc(y_seq, 1)
                        y_count[0] += 1

            y_count = [0]

            def update_x(n):
                cols = slice(n * COLS, (n + 1) * COLS)
                for t in range(TOK):
                    done = vector.scalar_tensor_tensor(out=xs[:, t, cols], in0=ys[:, t, cols],
                                                       scalar=yrstd[:, t:t + 1], in1=xs[:, t, cols],
                                                       op0=ALU.mult, op1=ALU.add)
                done.then_inc(x_ready, 1)

            def y_factor(u, chunks_read=0):
                dve.wait_ge(y_seq, y_count[0])
                if chunks_read:
                    dve.wait_ge(acc_free, chunks_read)
                chain(vector.tensor_reduce(ymean[:], ysq[:], AX.X, ALU.add))
                vector.tensor_scalar(ymean[:], ymean[:], 1.0 / D, EPS, ALU.mult, ALU.add).then_inc(ymean_ready, 1)
                dve.wait_ge(yrstd_ready, u + 1)

            def turn_in(b, columns, step=lambda f: None, fills=range(KT // 2), banks=4):
                for f in fills:
                    step(f)
                    dve.wait_ge(at_hi_ready, 8 * b + f + 1)
                    for k in range(2):
                        kt = 2 * f + k
                        done = vector.scalar_tensor_tensor(
                            out=at_lo[:, kt, :], in0=ps[:, 4 + f % banks, k * S:(k + 1) * S],
                            scalar=columns[:, kt:kt + 1], in1=at_hi[:, kt, :].bitcast(F32),
                            op0=ALU.mult, op1=ALU.subtract)
                    done.then_inc(at_ready, 1)

            def turn_x(b, u, layer, norm, chunks_read=0):
                y_factor(u, chunks_read)
                update_x(0)
                update_x(1)

                def step(f):
                    if f in (1, 3):
                        update_x(2 + f // 2)

                turn_in(b, gain_t[:, (layer * 4 + norm) * KT:(layer * 4 + norm + 1) * KT], step)

            def relu_of(pr, u, k, parity):
                dve.wait_ge(split_free, chunk_done(pr))
                dve.wait_ge(xrstd_ready, k + 1)
                dve.wait_ge(rows_turned, u + 1)
                for t in range(TOK):
                    done = vector.tensor_scalar(relu_rows[:, t, :], ps[:, 2 * parity + t, :], xrstd[:, t:t + 1], 0.0,
                                                ALU.mult, ALU.max)
                done.then_inc(acc_free, 1)

            def mlp_layer(layer, k, boundary):
                up, down, wc = PR[f"up{layer}"], PR[f"down{layer}"], WC[f"up{layer}"]
                u0 = layer * N_UP

                wide_chunk(up, boundary)
                with dve.Fori(0, N_UP // 2 - 1) as i:
                    for j in (1, 2):
                        wide_chunk(i * 2 + (up + j), lambda: relu_of(i * 2 + (up + j - 1), i * 2 + (u0 + j - 1), k,
                                                                     (j - 1) % 2))
                wide_chunk(up + N_UP - 1, lambda: relu_of(up + N_UP - 2, u0 + N_UP - 2, k, 0))
                down_round(0, down, lambda: relu_of(up + N_UP - 1, u0 + N_UP - 1, k, 1))
                with dve.Fori(1, DOWN_ROUNDS) as i:
                    down_round(i, i + down, lambda: None)
                u, pr = 2 * layer + 1, down + DOWN_ROUNDS

                def first_half():
                    for n in range(2):
                        y_rows(u, n, [2 * n, 2 * n + 1], pr - 1, False)

                down_round(0, pr, first_half)
                with dve.Fori(1, DOWN_ROUNDS) as i:
                    down_round(i, i + pr, lambda: None)

            def second_half(u, pr):
                for n in range(2):
                    y_rows(u, 2 + n, [4 + 2 * n, 5 + 2 * n], pr, False)

            dve.sem_inc(acc_free, 2)
            for counted_from_one in (max_ready, o_ready):
                dve.sem_inc(counted_from_one, 1)

            dve.wait_ge(vectors_turned, 1)
            vector.tensor_copy(gain_t[:], ps[:, 7, 0:P]).then_inc(gain_t_ready, 1)
            vector.tensor_copy(misc_t[:], ps[:, 7, P:P + 3 * KT]).then_inc(misc_t_ready, 1)
            vector.tensor_copy(pe_t, ps[:, 7, 2 * P:2 * P + 2 * CMP_BLOCK]).then_inc(pe_t_ready, 1)

            own = Steps(dve, dve_seq)

            def part_rows(rows, part, g):
                dve.wait_ge(split_free, PIECES * 4 * g + chunk_done(PR["gated"] + part))
                dve.wait_ge(xrstd_ready, 3)
                for t in range(TOK):
                    done = vector.tensor_scalar(rows[:, t, :], ps[:, 2 * (part % 2) + t, :], xrstd[:, t:t + 1], None,
                                                ALU.mult)
                done.then_inc(acc_free, 1)

            def sides(j, g):
                dve.wait_ge(decay_ready, g * (LEVELS + 1) + (j + 1))
                m = CHUNK >> j if j < LEVELS else P
                (to_first, to_second), (keys, _), (_, queries) = (halves(a, m) for a in
                                                                  (decay[:, j % 2], key[:], query[:]))
                vector.tensor_tensor(to_first, to_first, keys, ALU.mult)
                far = to_second if j == LEVELS else far_q[:, j % 2].rearrange("p (n m) -> p n m", m=m)
                vector.tensor_tensor(far, to_second, queries, ALU.mult).then_inc(sides_ready, 1)

            def take_level(j, g):
                dve.wait_ge(level_acc, g * (LEVELS + 1) + (j + 1))
                if j < LEVELS:
                    dve.sem_inc(dve_waited, 1)
                    m = CHUNK >> j
                    n = CHUNK // m
                    where = masks[:, j].bitcast(U32).rearrange("p (n m) -> p n m", m=m).unsqueeze(1).broadcast_to((P, R * TOK, n, m))
                    done = vector.copy_predicated(
                        mix_t[:].rearrange("p a (n two m) -> p a n two m", two=2, m=m)[:, :, :, 1, :], where,
                        ps[:, 6 + j % 2, :].rearrange("p (a n m) -> p a n m", a=R * TOK, m=m))
                else:
                    done = vector.tensor_copy(cross_t[:].rearrange("p h t -> p (h t)"), ps[:, 7, :])
                done.then_inc(level_read, 1)

            def step(t, g):
                turned = ps[:, 4:6, :].rearrange("p b c -> p (b c)")
                if t == 11:
                    part_rows(relu_rows, 0, g)
                if t == 17:
                    vector.tensor_copy(lb_now[:], log_lb[:, bass.ds(g * R, R)])
                    vector.tensor_copy(rest_now[:], log_rest[:, bass.ds(g * R, R)])
                    dve.wait_ge(f_log, g + 1)
                    vector.scalar_tensor_tensor(out=log_b[:], in0=turned, scalar=0.0, in1=log_a[:], op0=ALU.min,
                                                op1=ALU.subtract)
                    vector.scalar_tensor_tensor(out=log_c[:], in0=turned, scalar=0.0, in1=log_a[:], op0=ALU.max,
                                                op1=ALU.add).then_inc(f_read, 1)
                if t == 18:
                    dve.wait_ge(f_read, g + 1)
                    for op1, to, signal in ((ALU.subtract, log_a, odds_ready), (ALU.max, log_b, dve_seq)):
                        for h in range(R):
                            cols = slice(h * S, (h + 1) * S)
                            done = vector.tensor_scalar(to[:, cols], log_b[:, cols], rest_now[:, h:h + 1],
                                                        lb_now[:, h:h + 1], ALU.add, op1)
                        if signal is odds_ready:
                            done.then_inc(odds_ready, 1)
                            dve.wait_ge(odds_ready, g + 1)
                        else:
                            own.link(done)
                if t == 19:
                    part_rows(relu_rows, 1, g)
                if t == 23:
                    dve.wait_ge(odds_log, g + 1)
                    own.link(vector.tensor_tensor(log_b[:], log_b[:], log_a[:], ALU.add))
                if t == 24:
                    vector.tensor_tensor_scan(run[:], restart[:], log_b[:], 0.0, ALU.mult, ALU.add
                                              ).then_inc(run_ready, 1)
                if t == 26:
                    dve.wait_ge(q_log, g + 1)
                    vector.scalar_tensor_tensor(out=log_c[:], in0=turned, scalar=0.0, in1=log_c[:], op0=ALU.min,
                                                op1=ALU.subtract).then_inc(q_min, 1)
                if t == 28:
                    dve.wait_ge(q_sigmoid, g + 1)
                    vector.tensor_tensor(query[:], turned, log_c[:], ALU.mult).then_inc(query_ready, 1)
                if t == 27:
                    part_rows(v_rows, 2, g)
                if t == 29:
                    dve.wait_ge(diag_acc, g + 1)
                    for n in range(2):
                        done = vector.tensor_tensor(mix_t[:, 4 * n:4 * n + 4],
                                                    ps[:, 6 + n, :].rearrange("p (a t) -> p a t", a=4),
                                                    ident[:].unsqueeze(1).broadcast_to((P, 4, P)), ALU.mult)
                    done.then_inc(diag_read, 1)
                if t == 35:
                    part_rows(relu_rows, 3, g)
                if t == 40:
                    dve.wait_ge(gate_log, g + 1)
                    vector.scalar_tensor_tensor(out=gate_rows[:], in0=relu_rows[:], scalar=0.0, in1=gate_rows[:],
                                                op0=ALU.min, op1=ALU.subtract).then_inc(gate_min, 1)
                if t == 42:
                    dve.wait_ge(gate_sigmoid, g + 1)
                    own.link(vector.tensor_tensor(gate_rows[:], gate_rows[:], relu_rows[:], ALU.mult))
                if t == 51:
                    dve.wait_ge(orstd_ready, g + 2)
                    for n in range(TOK * R):
                        t_, cols = n // R, slice((n % R) * P, (n % R + 1) * P)
                        done = vector.scalar_tensor_tensor(out=ys[:, t_, bass.ds(g * COLS + (n % R) * P, P)],
                                                           in0=ps[:, 6 + t_, cols], scalar=orstd[:, n:n + 1],
                                                           in1=gate_rows[:, t_, cols], op0=ALU.mult, op1=ALU.mult)
                    done.then_inc(mix_ready, 1)
                for j in range(LEVELS + 1):
                    if t == 30 + 2 * j:
                        sides(j, g)
                    if t == 32 + 2 * j:
                        take_level(j, g)

            def gated_layer():
                pr = PR["gated"]

                def into_gated():
                    second_half(1, pr - 1)
                    turn_x(2, 1, 1, 0)

                def before_the_scans():
                    dve.wait_ge(lb_ready, 1)
                    own.link(vector.memset(restart[:], 1.0))
                    own.link(vector.memset(restart[:].rearrange("p (n m) -> p n m", m=CHUNK)[:, :, 0:1], 0.0))
                    dve.wait_ge(masks_landed, 16)

                def parts(g, before):
                    for c in range(4):
                        for p in range(PIECES):
                            t = 8 * c + p
                            if before is not into_gated:
                                step(t + 32, before)
                            elif t == AHEAD:
                                before()
                            elif t == PIECES - 1:
                                before_the_scans()
                            step(t, g)
                            split_lo(p, g * 4 + (pr + c))

                parts(0, into_gated)
                with dve.Fori(1, G - 1) as g:
                    own.turn(g - 1, DVE_STEPS)
                    parts(g, g - 1)
                own.leave(G - 2, DVE_STEPS)
                parts(G - 1, G - 2)

                pr = PR["out1"]
                for q in range(2 * PIECES):
                    for f in range(KT // 2):
                        if FILL_SPLIT[f] == 32 + q:
                            turn_in(3, misc_t[:, 2 * KT:3 * KT], fills=(f,), banks=2)
                    for t in tail_steps(q):
                        step(t, G - 1)
                    split_lo(q % PIECES, pr + q // PIECES)
                wide_chunk(pr + 2, lambda: y_rows(2, 1, [2, 3], pr + 1, True),
                           lambda p: y_rows(2, 0, [0, 1], pr + 1, True) if p == 1 else None)
                wide_chunk(pr + 3, lambda: y_rows(2, 2, [0, 1], pr + 2, True))

                def into_mlp1():
                    y_rows(2, N_OUT - 1, [2, 3], PR["out1"] + N_OUT - 1, True)
                    turn_x(4, 2, 1, 2, 2 + WC["out1"] + N_OUT)

                mlp_layer(1, 3, into_mlp1)
                second_half(3, PR["down1"] + HALVES * DOWN_ROUNDS - 1)
                y_factor(3)
                for n in range(N_OUT):
                    update_x(n)

            def qkv_rows(c, pr, parity):
                dve.wait_ge(split_free, chunk_done(pr))
                dve.wait_ge(xrstd_ready, 1)
                for t in range(TOK):
                    done = vector.tensor_scalar(qkv[:, t, bass.ds(c * COLS, COLS)], ps[:, 2 * parity + t, :],
                                                xrstd[:, t:t + 1], None, ALU.mult)
                done.then_inc(acc_free, 1)

            wide_chunk(0, lambda: turn_in(0, gain_t[:, 0:KT]))

            dve.wait_ge(line_acc, 1)
            vector.tensor_copy(line_rows[0:H, 0:ND], ps[0:H, 2, 0:ND]).then_inc(line_ready, 1)
            dve.wait_ge(misc_t_ready, 1)
            low, high, top = misc_t[:, 0:KT], misc_t[:, KT:2 * KT], lb_tmp[:, 0]
            chain(vector.tensor_tensor(top, low, high, ALU.max))
            vector.tensor_tensor(lb_tmp[:, 1], low, top, ALU.subtract)
            vector.tensor_tensor(lb_tmp[:, 2], high, top, ALU.subtract).then_inc(lb_in, 1)
            dve.wait_ge(lb_out, 1)
            chain(vector.tensor_tensor(top, lb_tmp[:, 1], lb_tmp[:, 2], ALU.add))
            chain(vector.reciprocal(top, top))
            vector.tensor_tensor(lb_tmp[:, 1], lb_tmp[:, 1], top, ALU.mult)
            chain(vector.tensor_tensor(lb_tmp[:, 2], lb_tmp[:, 2], top, ALU.mult))
            chain(vector.tensor_tensor(lb_tmp[:, 2], lb_tmp[:, 1], lb_tmp[:, 2], ALU.add))
            chain(vector.tensor_tensor(lb_tmp[:, 2], lb_tmp[:, 2], lb_tmp[:, 1], ALU.subtract))
            chain(vector.tensor_scalar(lb_tmp[:, 3], lb_tmp[:, 2], -1.0, 1.0, ALU.mult, ALU.add))
            vector.tensor_scalar(lb_tmp[:, 4:6], lb_tmp[:, 2:4], TINY, NEG, ALU.is_lt, ALU.mult)
            chain(vector.tensor_scalar(lb_tmp[:, 0:2], lb_tmp[:, 2:4], TINY, None, ALU.max))
            vector.tensor_copy(lb_tmp[:, 2:4], lb_tmp[:, 0:2]).then_inc(lb_in, 1)
            dve.wait_ge(lb_out, 2)
            vector.tensor_tensor(log_lb[:], lb_tmp[:, 2], lb_tmp[:, 4], ALU.add)
            vector.tensor_tensor(log_rest[:], lb_tmp[:, 3], lb_tmp[:, 5], ALU.add).then_inc(lb_ready, 1)

            with dve.Fori(0, N_IN // 2 - 1) as i:
                for j in (1, 2):
                    wide_chunk(i * 2 + j, lambda: qkv_rows(i * 2 + (j - 1), i * 2 + (j - 1), (j - 1) % 2))
            wide_chunk(N_IN - 1, lambda: qkv_rows(N_IN - 2, N_IN - 2, 0))

            def gates():
                dve.wait_ge(gate_turned, 1)
                for t in range(TOK):
                    done = vector.tensor_scalar(gate_tmp[:, t], ps[:, 7, t * 3 * H:(t + 1) * 3 * H],
                                                xrstd[:, t:t + 1], None, ALU.mult)
                done.then_inc(gate_raw, 1)
                dve.wait_ge(gate_exp, 1)
                chain(vector.tensor_scalar(gate_tmp, gate_tmp, 1.0, None, ALU.add))
                chain(vector.reciprocal(gate_tmp, gate_tmp))
                for b in range(3):
                    done = vector.tensor_copy(gate[:, (b + 2) % 3], gate_tmp[:, :, b * H:(b + 1) * H])
                chain(done)
                dve.wait_ge(w2_landed, 32)
                chain(vector.tensor_tensor(gate[:, 2], gate[:, 2], any_sb[:].unsqueeze(2).broadcast_to((P, TOK, H)),
                                           ALU.mult))

            def compress():
                for i in range(2):
                    dve.wait_ge(raw_kv_turned, i + 1)
                    for a in range(2):
                        for b in range(2):
                            halves = ps[:, 2 * i + b, :].rearrange("p (g c r) -> p r g c", g=2, r=CMP_STRIDE)
                            offsets = pe_t[:, i * CMP_BLOCK + a * CMP_STRIDE:i * CMP_BLOCK + (a + 1) * CMP_STRIDE]
                            for gg in range(2):
                                done = vector.tensor_tensor(
                                    cmp_rows[i][:, a * CMP_STRIDE:(a + 1) * CMP_STRIDE, 2 * b + gg, :],
                                    halves[:, :, gg, a:a + NC],
                                    offsets.unsqueeze(2).broadcast_to((P, CMP_STRIDE, NC)), ALU.add)
                    done.then_inc(cmp_rows_ready, 1)
                gates()
                for i in range(2):
                    dve.wait_ge(cmp_done, i + 1)
                    chain(vector.tensor_copy(gelu_z, ps[0:G * NC, 4 + i, 0:P]))
                    chain(vector.tensor_tensor(gelu_u, gelu_z, gelu_z, ALU.mult))
                    chain(vector.tensor_scalar(gelu_u, gelu_u, 0.044715, 1.0, ALU.mult, ALU.add))
                    vector.tensor_tensor(gelu_u, gelu_u, gelu_z, ALU.mult).then_inc(gelu_in, 1)
                    dve.wait_ge(gelu_exp, i + 1)
                    chain(vector.tensor_scalar(gelu_e, gelu_e, 1.0, None, ALU.add))
                    chain(vector.reciprocal(gelu_e, gelu_e))
                    vector.tensor_tensor(gelu_out[:, i], gelu_z, gelu_e, ALU.mult).then_inc(gelu_ready, 1)
                    dve.wait_ge(gelu_turned, i + 1)
                    vector.tensor_copy(gelu_t[:, i], ps[:, 4 + i, P:P + G * NC]).then_inc(gelu_t_ready, 1)
                dve.wait_ge(cmp_out, 1)
                vector.tensor_copy(k_cmp[:], ps[:, 6, 0:G * NC]).then_inc(cmp_ready, 1)
                dve.wait_ge(cmp_out, 2)
                vector.tensor_copy(v_cmp[:].rearrange("c g d -> c (g d)"), ps[0:NC, 7, :]).then_inc(cmp_ready, 1)

            GRP = 13

            def stage_k(g):
                for t in range(TOK):
                    done = vector.tensor_copy(staged_kv[:, t, 0::2], kv_rows(t)[:, 0::2, bass.ds(g * P, P)])
                done.then_inc(k_staged, 1)

            def kv_rows(t):
                return qkv[:, t, H * P + 2 * G * P:].rearrange("p (s n) -> p s n", s=4)

            def take_k(turns):
                dve.wait_ge(k_turned, turns)
                vector.tensor_copy(k_t[:].rearrange("p b s -> p (b s)"), ps[:, 3, :]).then_inc(k_ready, 1)

            def group(g, last):
                n = [0]

                def link(done):
                    n[0] += 1
                    done.then_inc(grp_seq, 1)
                    dve.wait_ge(grp_seq, g * GRP + n[0])

                dve.wait_ge(o_acc, g + 1)
                vector.tensor_copy(v_cmp_now[:], v_cmp[:, bass.ds(g, 1), :].rearrange("c g d -> c (g d)"))
                for t in range(TOK):
                    done = vector.tensor_copy(staged_kv[:, t, 1::2], kv_rows(t)[:, 1::2, bass.ds(g * P, P)])
                done.then_inc(v_staged, 1)
                if not last:
                    stage_k(g + 1)
                over = lambda a: a.unsqueeze(3).broadcast_to((P, TOK, R, NC))
                dve.wait_ge(bias_landed, g * 16 + 16)
                for b in range(2):
                    if b == 1:
                        dve.wait_ge(cmp_logits, g + 1)
                        sums = ps[:, 7, 0:TOK * R * NC].rearrange("p (t h c) -> p t h c", t=TOK, h=R)
                        ends = bias.rearrange("p h (c s) -> p h c s", s=CMP_STRIDE)[:, :, 1:, CMP_STRIDE - 1]
                        vector.tensor_tensor(p_cmp[:, 1], sums[:, 1], ends, ALU.add)
                        vector.tensor_tensor(p_cmp[:, 0, :, 0:LOW_NC], sums[:, 0, :, 0:LOW_NC], ends[:, :, NC - LOW_NC:], ALU.add)
                        link(vector.memset(p_cmp[:, 0, :, LOW_NC:], NEG))
                        link(vector.tensor_reduce(stat[:, 2], p_cmp[:], AX.X, ALU.max))
                        vector.tensor_tensor(p_cmp[:], p_cmp[:], over(stat[:, 2]), ALU.subtract).then_inc(cmp_max, 1)
                    dve.wait_ge(logits_acc, g * 2 + (b + 1))
                    low = section0(logits[:, b])
                    vector.tensor_tensor(low, ps[:, BANKS[b], :].rearrange("p (h k) -> p h k", h=R), bias[:, :, P:S],
                                         ALU.add)
                    for m in range(2):
                        done = vector.tensor_tensor(
                            logits[:, b, 1 + m, :].rearrange("p (h k) -> p h k", h=2),
                            ps[:, BANKS[b] + 1 + m, :].rearrange("p (h k) -> p h k", h=2),
                            bias[:, 2 * m:2 * m + 2, :], ALU.add)
                    link(done)
                    vector.tensor_reduce(stat[:, b, 0], low, AX.X, ALU.max)
                    link(vector.tensor_reduce(stat[:, b, 1], logits[:, b, 1:3, :].rearrange(
                        "p m (h k) -> p (m h) k", h=2), AX.X, ALU.max))
                    vector.tensor_scalar(stat[:, b], stat[:, b], -1.0, None, ALU.mult).then_inc(max_ready, 1)
                dve.wait_ge(cmp_exp, g + 1)
                link(vector.tensor_reduce(total[:, 2], p_cmp[:], AX.X, ALU.add))
                link(vector.reciprocal(weight[:, 2], total[:, 2]))
                link(vector.tensor_tensor(weight[:, 2], weight[:, 2], gate[:, 2, :, bass.ds(g * R, R)], ALU.mult))
                vector.tensor_tensor(p_cmp[:], p_cmp[:], over(weight[:, 2]), ALU.mult).then_inc(p_cmp_ready, 1)
                for b in range(2):
                    dve.wait_ge(exp_ready, g * 2 + (b + 1))
                    link(vector.reciprocal(weight[:, b], total[:, b]))
                    link(vector.tensor_tensor(weight[:, b], weight[:, b], gate[:, b, :, bass.ds(g * R, R)], ALU.mult))
                    low = section0(logits[:, b])
                    vector.tensor_tensor(low, low, weight[:, b, 0].unsqueeze(2).broadcast_to((P, R, P)), ALU.mult)
                    for m in range(2):
                        high = logits[:, b, 1 + m, :].rearrange("p (h k) -> p h k", h=2)
                        done = vector.tensor_tensor(high, high, weight[:, b, 1, 2 * m:2 * m + 2].unsqueeze(2)
                                                    .broadcast_to((P, 2, S)), ALU.mult)
                    done.then_inc(p_ready, 1)
                if not last:
                    take_k(g + 2)
                dve.wait_ge(o_hi_ready, g + 1)
                vector.tensor_tensor(at_lo[:, bass.ds(g * R, R), :].rearrange("p k s -> p (k s)"),
                                     ps[:, 6:8, :].rearrange("p b c -> p (b c)"),
                                     at_hi[:, bass.ds(g * R, R), :].rearrange("p k s -> p (k s)").bitcast(F32),
                                     ALU.subtract).then_inc(o_ready, 1)
                return n[0]

            def attention():
                dve.wait_ge(wg_hi_ready, 1)
                vector.tensor_tensor(wg_lo[:], wg_raw, wg_hi[:].bitcast(F32), ALU.subtract).then_inc(wg_ready, 1)
                qkv_rows(N_IN - 1, N_IN - 1, 1)
                dve.wait_ge(acc_free, 2 + N_IN)
                dve.wait_ge(gate_acc, 1)
                vector.tensor_copy(gate_t, ps[0:3 * H, 6, 0:S]).then_inc(gate_t_ready, 1)
                compress()
                dve.wait_ge(cmp_ready, 2)
                stage_k(0)
                take_k(1)
                with dve.Fori(0, G - 1) as g:
                    steps = group(g, False)
                assert steps == group(G - 1, True) == GRP, steps

            def wide_rows_out(name, u):
                for c in range(N_OUT):
                    pr = PR[name] + c
                    wide_chunk(pr, lambda: y_rows(u, c - 1, [2 * ((c - 1) % 2), 2 * ((c - 1) % 2) + 1], pr - 1, True)
                               if c else None)

            attention()
            wide_rows_out("out", 0)

            def into_mlp0():
                y_rows(0, N_OUT - 1, [2, 3], PR["out"] + N_OUT - 1, True)
                turn_x(1, 0, 0, 2, 2 + WC["out"] + N_OUT)

            mlp_layer(0, 1, into_mlp0)
            gated_layer()

        @block.tensor
        def _(pe):
            tensor = nc.tensor

            def three_passes(acc, kt, t, hi, lo, start, stop):
                rows = slice(t * P, (t + 1) * P)
                tensor.matmul(acc, at_hi[:, kt, rows], hi, start=start, stop=False)
                tensor.matmul(acc, at_lo[:, kt, rows], hi, start=False, stop=False)
                return tensor.matmul(acc, at_hi[:, kt, rows], lo, start=False, stop=stop)

            def wide_chunk(pr, wc, parity, before=lambda p: None, after=lambda p: None):
                pe.wait_ge(acc_free, wc + 1)
                for p in range(PIECES):
                    before(p)
                    pe.wait_ge(lo_ready, PIECES * pr + (p + 1))
                    for k in range(2):
                        cols = slice(k * COLS, (k + 1) * COLS)
                        for t in range(TOK):
                            done = three_passes(ps[:, 2 * parity + t, :], 2 * p + k, t, w_hi[:, p % SPLITS, cols],
                                                w_lo[:, p % SPLITS, cols], p + k == 0, 2 * p + k == KT - 1)
                    done.then_inc(split_free, 1)
                    after(p)

            def down_round(half, pr, first, last, after=lambda p: None):
                for p in range(PIECES):
                    pe.wait_ge(lo_ready, PIECES * pr + (p + 1))
                    for n in range(2):
                        cols = slice(n * COLS, (n + 1) * COLS)
                        for t in range(TOK):
                            done = three_passes(ps[:, 4 * half + 2 * n + t, :], p, t, w_hi[:, p % SPLITS, cols],
                                                w_lo[:, p % SPLITS, cols], first and p == 0,
                                                last and p == PIECES - 1)
                    done.then_inc(split_free, 1)
                    after(p)

            def turn(b, f, source, banks=4):
                if f >= banks:
                    pe.wait_ge(at_ready, 8 * b + f - banks + 1)
                for k in range(2):
                    for t in range(TOK):
                        kt = 2 * f + k
                        done = tensor.transpose(ps[:, 4 + f % banks, k * S + t * P:k * S + (t + 1) * P],
                                                source[:, t, kt * P:(kt + 1) * P], ident[:])
                done.then_inc(xt_ready, 1)

            def turned_chunk(b, pr, wc, source, wait_source, after=lambda p: None):
                def before(p):
                    for f in ((0, 1, 2, 3), (4, 5), (6, 7), (), (), (), (), ())[p]:
                        wait_source(f)
                        turn(b, f, source)
                    pe.wait_ge(at_ready, 8 * b + p + 1)
                wide_chunk(pr, wc, 0, before, after)

            def turn_hidden(wc, u):
                pe.wait_ge(acc_free, wc + 2)
                pe.wait_ge(hidden_ready, u + 1)
                for j in range(4):
                    for t in range(TOK):
                        done = tensor.transpose(ps[:, 4 + j // 2, (j % 2) * S + t * P:(j % 2) * S + (t + 1) * P],
                                                relu_rows[:, t, j * P:(j + 1) * P], ident[:])
                done.then_inc(rows_turned, 1)

            def mlp_layer(layer, b, update):
                up, down, wc, u0 = PR[f"up{layer}"], PR[f"down{layer}"], WC[f"up{layer}"], layer * N_UP
                turned_chunk(b, up, wc, xs, lambda f: pe.wait_ge(x_ready, N_OUT * update + f // 2 + 1))

                def at(piece, work):
                    return lambda p: work() if p == piece else None

                with pe.Fori(0, N_UP // 2 - 1) as i:
                    for j in (1, 2):
                        wide_chunk(i * 2 + (up + j), i * 2 + (wc + j), j % 2,
                                   after=at(1, lambda: turn_hidden(i * 2 + (wc + j), i * 2 + (u0 + j - 1))))
                wide_chunk(up + N_UP - 1, wc + N_UP - 1, 1,
                           after=at(1, lambda: turn_hidden(wc + N_UP - 1, u0 + N_UP - 2)))
                pe.wait_ge(acc_free, wc + N_UP + 2)
                down_round(0, down, True, False, after=at(1, lambda: turn_hidden(wc + N_UP, u0 + N_UP - 1)))
                with pe.Fori(1, DOWN_ROUNDS - 1) as i:
                    down_round(0, i + down, False, False)
                down_round(0, down + DOWN_ROUNDS - 1, False, True)
                down += DOWN_ROUNDS
                pe.wait_ge(hidden_ready, u0 + N_UP + 1)
                down_round(1, down, True, False)
                with pe.Fori(1, DOWN_ROUNDS - 1) as i:
                    down_round(1, i + down, False, False)
                down_round(1, down + DOWN_ROUNDS - 1, False, True)

            def turn_part(g, part, ready):
                pe.wait_ge(acc_free, g * 4 + (WC["gated"] + part + 3))
                for h in range(R):
                    for t in range(TOK):
                        done = tensor.transpose(ps[:, 4 + h // 2, (h % 2) * S + t * P:(h % 2) * S + (t + 1) * P],
                                                relu_rows[:, t, h * P:(h + 1) * P], ident[:])
                done.then_inc(ready, 1)

            def step(t, g):
                if t == 9:
                    pe.wait_ge(query_ready, g)
                    turn_part(g, 0, f_turned)
                if t == 18:
                    pe.wait_ge(f_read, g + 1)
                    turn_part(g, 1, q_turned1)
                if t == 25:
                    pe.wait_ge(key_ready, g + 1)
                    pe.wait_ge(query_ready, g + 1)
                    pe.wait_ge(mix_ready, g)
                    for a in range(R * TOK):
                        done = tensor.matmul(ps[:, 6 + a // 4, (a % 4) * P:(a % 4 + 1) * P], key[:, a * P:(a + 1) * P],
                                             query[:, a * P:(a + 1) * P], start=True, stop=True)
                    done.then_inc(diag_acc, 1)
                if 27 <= t <= 27 + 2 * LEVELS and t % 2 == 1:
                    j = (t - 27) // 2
                    pe.wait_ge(sides_ready, g * (LEVELS + 1) + (j + 1))
                    pe.wait_ge(diag_read, g + 1)
                    if j >= 2:
                        pe.wait_ge(level_read, g * (LEVELS + 1) + (j - 1))
                    if j < LEVELS:
                        half = P // 2
                        for a in range(R * TOK):
                            done = tensor.matmul(ps[:, 6 + j % 2, a * half:(a + 1) * half],
                                                 decay[:, j % 2, a * P:(a + 1) * P],
                                                 far_q[:, j % 2, a * half:(a + 1) * half], start=True, stop=True)
                    else:
                        for h in range(R):
                            done = tensor.matmul(ps[:, 7, h * P:(h + 1) * P], decay[:, 1, h * S:h * S + P],
                                                 decay[:, 1, h * S + P:(h + 1) * S], start=True, stop=True)
                    done.then_inc(level_acc, 1)
                if t == 44:
                    pe.wait_ge(level_read, g * (LEVELS + 1) + (LEVELS + 1))
                    pe.wait_ge(acc_free, g * 4 + (WC["gated"] + 2 + 3))
                    for h in range(R):
                        cols = slice(h * P, (h + 1) * P)
                        tensor.matmul(ps[:, 6, cols], mix_t[:, h * TOK, :], v_rows[:, 0, cols], start=True, stop=True)
                        tensor.matmul(ps[:, 7, cols], cross_t[:, h, :], v_rows[:, 0, cols], start=True, stop=False)
                        done = tensor.matmul(ps[:, 7, cols], mix_t[:, h * TOK + 1, :], v_rows[:, 1, cols],
                                             start=False, stop=True)
                    done.then_inc(mix_acc, 1)

            def gated_layer():
                pr, wc = PR["gated"], WC["gated"]
                for c in range(4):
                    after = lambda p: step(8 * c + p, 0)
                    if c == 0:
                        turned_chunk(2, pr, wc, xs, lambda f: pe.wait_ge(x_ready, N_OUT + f // 2 + 1))
                    else:
                        wide_chunk(pr + c, wc + c, c % 2, after=after)

                def turn_output(f):
                    if f == 0:
                        pe.wait_ge(mix_ready, G - 1)
                    turn(3, f, ys, 2)

                def parts(g):
                    for c in range(4):
                        def after(p):
                            step(8 * c + p + 32, g - 1)
                            step(8 * c + p, g)
                            if isinstance(g, int) and 8 * c + p in FILL_TURNED:
                                turn_output(FILL_TURNED.index(8 * c + p))
                        wide_chunk(g * 4 + (pr + c), g * 4 + (wc + c), c % 2, after=after)

                with pe.Fori(1, G - 1) as g:
                    parts(g)
                parts(G - 1)
                pr, wc = PR["out1"], WC["out1"]
                for q in range(2 * PIECES):
                    if q == LATE_TURNED:
                        pe.wait_ge(mix_ready, G)
                        for f in LATE_FILLS:
                            turn(3, f, ys, 2)
                    c, quarter = PAIR[q // 2]
                    if quarter == 0 and q % 2 == 0:
                        pe.wait_ge(acc_free, wc + c + 1)
                    pair_of_tiles = 2 * quarter + q % 2
                    pe.wait_ge(at_ready, 8 * 3 + pair_of_tiles + 1)
                    pe.wait_ge(lo_ready, PIECES * pr + (q + 1))
                    for k in range(2):
                        cols = slice(k * COLS, (k + 1) * COLS)
                        for t in range(TOK):
                            done = three_passes(ps[:, 2 * c + t, :], 2 * pair_of_tiles + k, t, w_hi[:, q % SPLITS, cols],
                                                w_lo[:, q % SPLITS, cols], pair_of_tiles + k == 0,
                                                2 * pair_of_tiles + k == KT - 1)
                    done.then_inc(split_free, 1)
                    for t in tail_steps(q):
                        step(t, G - 1)
                    if 32 + q in FILL_TURNED:
                        turn_output(FILL_TURNED.index(32 + q))
                for c in range(2, N_OUT):
                    wide_chunk(PR["out1"] + c, WC["out1"] + c, c % 2)
                mlp_layer(1, 4, 2)

            pe.sem_inc(split_free, SPLITS)
            for counted_from_one in (o_acc, rows_turned):
                pe.sem_inc(counted_from_one, 1)

            pe.wait_ge(rows_landed, 80)
            tensor.transpose(ps[:, 7, 0:P], gain_rows, ident[:])
            tensor.transpose(ps[:, 7, P:P + 3 * KT], misc_rows, ident[0:3 * KT, 0:3 * KT])
            tensor.transpose(ps[:, 7, 2 * P:2 * P + 2 * CMP_BLOCK], pe_rows, ident[0:2 * CMP_BLOCK, 0:2 * CMP_BLOCK]
                             ).then_inc(vectors_turned, 1)

            def bias_by_distance():
                pe.wait_ge(table_ready, 32)
                tensor.matmul(ps[0:H, 2, 0:ND], table, rows_back, start=True, stop=True).then_inc(line_acc, 1)

            def rows_are_in(f):
                if f == 0:
                    pe.wait_ge(x_landed, 16 * TOK)
                if f == 3:
                    pe.wait_ge(pe_t_ready, 1)

            turned_chunk(0, 0, 0, xs, rows_are_in, lambda p: bias_by_distance() if p == 4 else None)
            pe.wait_ge(line_ready, 1)
            with pe.Fori(0, N_IN // 2 - 1) as i:
                for j in (1, 2):
                    wide_chunk(i * 2 + j, i * 2 + j, j % 2)
            wide_chunk(N_IN - 1, N_IN - 1, 1)

            pe.wait_ge(wg_ready, 1)
            for kt in range(KT):
                tensor.matmul(ps[0:3 * H, 6, 0:S], wg_hi[:, kt, :], at_hi[:, kt, :], start=kt == 0, stop=False)
                tensor.matmul(ps[0:3 * H, 6, 0:S], wg_lo[:, kt, :], at_hi[:, kt, :], start=False, stop=False)
                done = tensor.matmul(ps[0:3 * H, 6, 0:S], wg_hi[:, kt, :], at_lo[:, kt, :], start=False,
                                     stop=kt == KT - 1)
            done.then_inc(gate_acc, 1)
            pe.wait_ge(acc_free, 2 + N_IN)
            for i in range(2):
                for g in range(G):
                    for t in range(TOK):
                        first = (H + (i * G) + g) * P
                        done = tensor.transpose(ps[:, 2 * i + g // 2, (g % 2) * S + t * P:(g % 2) * S + (t + 1) * P],
                                                qkv[:, t, first:first + P], ident[:])
                done.then_inc(raw_kv_turned, 1)
            pe.wait_ge(gate_t_ready, 1)
            for t in range(TOK):
                done = tensor.transpose(ps[:, 7, t * 3 * H:(t + 1) * 3 * H], gate_t[:, t * P:(t + 1) * P],
                                        ident[0:3 * H, 0:3 * H])
            done.then_inc(gate_turned, 1)
            for i in range(2):
                pe.wait_ge(cmp_rows_ready, i + 1)
                for j in (2 * i, 2 * i + 1):
                    pe.wait_ge(w_landed[j], 16 * (N_IN + 1))
                for l in range(CMP_BLOCK):
                    j = 2 * i + l // 16
                    done = tensor.matmul(ps[0:G * NC, 4 + i, 0:P], cmp_rows[i][:, l].rearrange("p g c -> p (g c)"),
                                         raw[:, j, (l % 16) * P:(l % 16 + 1) * P], start=l == 0,
                                         stop=l == CMP_BLOCK - 1)
                done.then_inc(cmp_done, 1)
            for i in range(2):
                pe.wait_ge(gelu_ready, i + 1)
                tensor.transpose(ps[:, 4 + i, P:P + G * NC], gelu_out[:, i], ident[0:G * NC, 0:G * NC]
                                 ).then_inc(gelu_turned, 1)
            pe.wait_ge(w2_landed, 32)
            pe.wait_ge(gelu_t_ready, 1)
            tensor.matmul(ps[:, 6, 0:G * NC], w2[:, 0, :], gelu_t[:, 0], start=True, stop=True).then_inc(cmp_out, 1)
            pe.wait_ge(gelu_t_ready, 2)
            for g in range(G):
                done = tensor.matmul(ps[0:NC, 7, g * P:(g + 1) * P], gelu_t[:, 1, g * NC:(g + 1) * NC], w2[:, 1, :],
                                     start=True, stop=True)
            done.then_inc(cmp_out, 1)
            pe.wait_ge(cmp_ready, 2)

            def turn_qk(turns):
                pe.wait_ge(q_staged, turns)
                for h in range(R):
                    for t in range(TOK):
                        done = tensor.transpose(ps[:, 4 + h // 2, (h % 2) * S + t * P:(h % 2) * S + (t + 1) * P],
                                                staged_q[:, t, h * P:(h + 1) * P], ident[:])
                done.then_inc(q_turned, 1)
                pe.wait_ge(k_staged, turns)
                for b in range(2):
                    for t in range(TOK):
                        done = tensor.transpose(ps[:, 3, b * S + t * P:b * S + (t + 1) * P], staged_kv[:, t, 2 * b, :],
                                                ident[:])
                done.then_inc(k_turned, 1)

            def values(b):
                both, late = p_t_of(b)[:, 0:R * S], p_t_of(b)[:, R * S:R * S + R * P]
                for n in range(2):
                    acc = ps[:, 6 + n, :]
                    tensor.matmul(acc, staged_kv[:, 0, 2 * b + 1, :], both[:, n * COLS:(n + 1) * COLS],
                                  start=b == 0, stop=False, skip_group_check=True)
                    done = tensor.matmul(acc.rearrange("p (h s) -> p h s", h=2)[:, :, P:S],
                                         staged_kv[:, 1, 2 * b + 1, :], late[:, n * S:(n + 1) * S],
                                         start=False, stop=b == 1, skip_group_check=True)
                return done

            def group(g, last):
                pe.wait_ge(q_ready, g + 1)
                pe.wait_ge(k_ready, g + 1)
                for b in range(2):
                    if b == 1:
                        pe.wait_ge(o_ready, g + 1)
                        for t in range(TOK):
                            for h in range(R):
                                at = (t * R + h) * NC
                                done = tensor.matmul(ps[:, 7, at:at + NC], q_t[:, h, t * P:(t + 1) * P],
                                                     k_cmp[:, bass.ds(g * NC, NC)], start=True, stop=True)
                        done.then_inc(cmp_logits, 1)
                    for h in range(R):
                        tensor.matmul(ps[:, BANKS[b], h * P:(h + 1) * P], q_t[:, h, 0:P], k_t[:, b, 0:P],
                                      start=True, stop=True)
                        done = tensor.matmul(ps[:, BANKS[b] + 1 + h // 2, (h % 2) * S:(h % 2 + 1) * S], q_t[:, h, P:S],
                                             k_t[:, b, :], start=True, stop=True)
                    done.then_inc(logits_acc, 1)
                pe.wait_ge(p_cmp_ready, g + 1)
                for h in range(R):
                    for t in range(TOK):
                        done = tensor.transpose(ps[0:NC, 6 + h // 2, (h % 2) * S + t * P:(h % 2) * S + (t + 1) * P],
                                                p_cmp[:, t, h, :], ident[:])
                done.then_inc(p_cmp_turned, 1)
                for b in range(2):
                    pe.wait_ge(p_ready, g * 2 + (b + 1))
                    for h in range(R):
                        high = ps[:, BANKS[b] + h // 2, :]
                        base = (h % 2) * S
                        tensor.transpose(high[:, base:base + P], section(logits[:, b], 0, h), ident[:])
                        above = section(logits[:, b], 1, h)
                        tensor.transpose(high[:, base + P:base + S], above[:, 0:P], ident[:])
                        done = tensor.transpose(ps[:, BANKS[b] + 2, h * P:(h + 1) * P], above[:, P:S], ident[:])
                    done.then_inc(p_turned, 1)
                pe.wait_ge(p_t_ready, g * 2 + 1)
                if not last:
                    turn_qk(g + 2)
                pe.wait_ge(v_staged, g + 1)
                pe.wait_ge(pc_t_ready, g + 1)
                values(0)
                for n in range(2):
                    tensor.matmul(ps[:, 6 + n, :], v_cmp_now[:], pc_t[:, n * COLS:(n + 1) * COLS], start=False,
                                  stop=False, skip_group_check=True)
                pe.wait_ge(p_t_ready, g * 2 + 2)
                values(1).then_inc(o_acc, 1)

            turn_qk(1)
            with pe.Fori(0, G - 1) as g:
                group(g, False)
            group(G - 1, True)
            pe.wait_ge(o_ready, G + 1)

            for c in range(N_OUT):
                wide_chunk(PR["out"] + c, WC["out"] + c, c % 2)
            mlp_layer(0, 1, 0)
            gated_layer()


_INS = ["x", "norm_g", "rel_table", "nsa_w_in", "nsa_cmp_pe", "nsa_cmp_w1", "nsa_cmp_w2", "nsa_w_out", "hgrn_w_in",
        "hgrn_lb", "hgrn_onorm", "hgrn_w_out", "mlp_w_up", "mlp_w_down"]


def shape_constants(seq):
    dist = np.arange(-(seq - 1), seq)
    n = np.maximum(dist, 0)
    exact = BUCKETS // 2
    far = exact + (np.log(np.maximum(n, 1) / exact) / np.log(MAX_DIST / exact) * (BUCKETS - exact)).astype(np.int64)
    bucket = np.where(n < exact, n, np.minimum(far, BUCKETS - 1))
    rows = np.zeros((BUCKETS + 1, dist.size), np.float32)
    rows[bucket, np.arange(dist.size)] = 1.0
    rows[:, dist < 0] = 0.0
    rows[BUCKETS, dist < 0] = NEG
    pos = np.arange(seq).reshape(-1, P).T
    key, query = np.arange(P)[:, None], np.arange(P)[None, :]
    levels = []
    for j in range(LEVELS):
        m = CHUNK >> j
        pairs = (key // (2 * m) == query // (2 * m)) & (key // m % 2 == 0)
        levels.append(pairs[:, np.arange(P) // m % 2 == 1])
    return {
        "identity": np.eye(P, dtype=np.float32),
        "bucket_rows_back": np.ascontiguousarray(rows[:, ::-1]),
        "any_cmp": (pos >= CMP_BLOCK - 1).astype(np.float32),
        "level_masks": np.stack(levels, 1).astype(np.float32),
    }


def kernel(**inputs):
    import concourse.bacc as bacc
    from concourse.bass_utils import run_bass_kernel_spmd

    nc = bacc.Bacc("TRN2", target_bir_lowering=False, num_devices=1)
    arrays, args = {}, []
    values = [(name, np.ascontiguousarray(inputs[name])) for name in _INS]
    values += list(shape_constants(inputs["x"].shape[1]).items())
    for name, a in values:
        arrays[f"in_{name}"] = a
        args.append(nc.dram_tensor(f"in_{name}", a.shape, mybir.dt.from_np(a.dtype), kind="ExternalInput").ap())
    args.append(nc.dram_tensor("out_0", inputs["x"].shape, F32, kind="ExternalOutput").ap())
    trunk_kernel(nc, *args)
    result = run_bass_kernel_spmd(nc, [arrays], core_ids=[0])
    return result.results[0]["out_0"]
```
